# Optimizing a Trainium2 kernel written in Bass

```python
import jax, jax.numpy as jnp
from jax import lax
import numpy as np
import math

D_MODEL = 1024
BATCH = 1
SEQ = 256
DEPTH = 2

CHUNK = 64
EPS = 1e-6
ROPE_BASE = 10000.0
RET_HEADS = 4
RET_DIM = 128
RET_VDIM = 128
ATT_HEADS = 8
ATT_DIM = 64
ATT_LEFT_CHUNKS = 8
REL_CLIP = 128
REL_SIZE = CHUNK - 1 + REL_CLIP + 1
SB_HEADS = 16
SB_DIM = 64
SB_BLOCK = 128
N_EXPERTS = 16
N_GROUPS = 4
TOP_K = 2
D_EXPERT = 512

N_EVEN = (DEPTH + 1) // 2
N_ODD = DEPTH // 2
RET_W = RET_HEADS * RET_DIM
RET_VW = RET_HEADS * RET_VDIM
ATT_W = ATT_HEADS * ATT_DIM
EVEN_IN = 2 * RET_W + 2 * RET_VW + 3 * ATT_W
EVEN_MIX = RET_VW + ATT_W
EVEN_SPLITS = (RET_W, 2 * RET_W, 2 * RET_W + RET_VW, 2 * RET_W + 2 * RET_VW,
               2 * RET_W + 2 * RET_VW + ATT_W, 2 * RET_W + 2 * RET_VW + 2 * ATT_W)
SB_W = SB_HEADS * SB_DIM
ODD_IN = 3 * SB_W


def rms_norm(x, gain):
    xf = x.astype(jnp.float32)
    y = xf * lax.rsqrt(jnp.mean(xf * xf, axis=-1, keepdims=True) + EPS)
    return (y * gain.astype(jnp.float32)).astype(x.dtype)

def head_rms(x):
    xf = x.astype(jnp.float32)
    return xf * lax.rsqrt(jnp.mean(xf * xf, axis=-1, keepdims=True) + EPS)

def rotary(x, pos):
    d = x.shape[-1]
    inv = ROPE_BASE ** (-jnp.arange(0, d, 2, dtype=jnp.float32) / d)
    ang = pos.astype(jnp.float32)[:, None] * inv[None, :]
    cos = jnp.cos(ang)[None, :, None, :]
    sin = jnp.sin(ang)[None, :, None, :]
    x1, x2 = jnp.split(x.astype(jnp.float32), 2, axis=-1)
    return jnp.concatenate([x1 * cos - x2 * sin, x1 * sin + x2 * cos], axis=-1).astype(x.dtype)

def retention(q, k, v):
    B_, S, H, dk = q.shape
    dv = v.shape[-1]
    nc = S // CHUNK
    log_g = jnp.log(1.0 - 2.0 ** (-5.0 - jnp.arange(H, dtype=jnp.float32)))
    idx = jnp.arange(CHUNK, dtype=jnp.float32)
    intra_dec = jnp.exp(log_g[:, None, None] * jnp.abs(idx[:, None] - idx[None, :]))
    q_dec = jnp.exp(log_g[:, None] * (idx[None, :] + 1.0))
    k_dec = jnp.exp(log_g[:, None] * (CHUNK - 1.0 - idx[None, :]))
    chunk_dec = jnp.exp(log_g * CHUNK)
    qc = q.astype(jnp.float32).reshape(B_, nc, CHUNK, H, dk)
    kc = k.astype(jnp.float32).reshape(B_, nc, CHUNK, H, dk)
    vc = v.astype(jnp.float32).reshape(B_, nc, CHUNK, H, dv)
    scores = jnp.einsum('bnihd,bnjhd->bnhij', qc, kc) * intra_dec
    o_intra = jnp.einsum('bnhij,bnjhe->bnihe', scores, vc)
    kv = jnp.einsum('bnjhd,hj,bnjhe->bnhde', kc, k_dec, vc)

    def step(state, kv_n):
        return state * chunk_dec[None, :, None, None] + kv_n, state

    init = jnp.zeros((B_, H, dk, dv), jnp.float32)
    _, prev = lax.scan(step, init, jnp.moveaxis(kv, 1, 0))
    prev = jnp.moveaxis(prev, 0, 1)
    o_cross = jnp.einsum('bnihd,hi,bnhde->bnihe', qc, q_dec, prev)
    return (o_intra + o_cross).reshape(B_, S, H, dv)

def chunk_attention(q, k, v, rel_bias):
    B_, S, H, d = q.shape
    nc = S // CHUNK
    band = ATT_LEFT_CHUNKS + 1

    def gather_band(t):
        tc = t.reshape(B_, nc, CHUNK, H, d)
        tp = jnp.pad(tc, ((0, 0), (ATT_LEFT_CHUNKS, 0), (0, 0), (0, 0), (0, 0)))
        return jnp.concatenate([tp[:, j:j + nc] for j in range(band)], axis=2)

    qc = q.reshape(B_, nc, CHUNK, H, d)
    kb = gather_band(k)
    vb = gather_band(v)
    kk = np.arange(band * CHUNK)
    dist = ATT_LEFT_CHUNKS * CHUNK + np.arange(CHUNK)[:, None] - kk[None, :]
    rel_idx = np.clip(dist, -(CHUNK - 1), REL_CLIP) + (CHUNK - 1)
    bias = rel_bias[:, rel_idx].astype(jnp.float32)
    valid = (np.arange(nc)[:, None] - ATT_LEFT_CHUNKS + kk[None, :] // CHUNK) >= 0
    s = jnp.einsum('bnihd,bnkhd->bnhik', qc, kb).astype(jnp.float32) * (d ** -0.5)
    s = s + bias[None, None]
    s = jnp.where(valid[None, :, None, None, :], s, -jnp.inf)
    p = jax.nn.softmax(s, axis=-1)
    o = jnp.einsum('bnhik,bnkhd->bnihd', p, vb.astype(jnp.float32))
    return o.reshape(B_, S, H, d).astype(q.dtype)

def stick_breaking(q, k, v):
    B_, S, H, d = q.shape
    scale = d ** -0.5
    outs = []
    for blk in range(S // SB_BLOCK):
        q0 = blk * SB_BLOCK
        kend = q0 + SB_BLOCK
        z = jnp.einsum('bihd,bjhd->bhij', q[:, q0:kend], k[:, :kend]).astype(jnp.float32) * scale
        causal = jnp.arange(kend)[None, :] < (q0 + jnp.arange(SB_BLOCK))[:, None]
        log_beta = jax.nn.log_sigmoid(z)
        log_1mb = jnp.where(causal, jax.nn.log_sigmoid(-z), 0.0)
        acc = lax.cumsum(log_1mb, axis=3, reverse=True) - log_1mb
        a = jnp.where(causal, jnp.exp(log_beta + acc), 0.0)
        outs.append(jnp.einsum('bhij,bjhd->bihd', a, v[:, :kend].astype(jnp.float32)))
    return jnp.concatenate(outs, axis=1).astype(q.dtype)

def even_mixer(h, w_in, w_out, q_norm_g, k_norm_g, rel_bias, pos):
    B_, S, _ = h.shape
    proj = h @ w_in
    rq, rk, rv, rg, aq, ak, av = jnp.split(proj, EVEN_SPLITS, axis=-1)
    rq = rotary(rq.reshape(B_, S, RET_HEADS, RET_DIM), pos)
    rk = rotary(rk.reshape(B_, S, RET_HEADS, RET_DIM), pos) * (RET_DIM ** -0.5)
    ret = retention(rq, rk, rv.reshape(B_, S, RET_HEADS, RET_VDIM))
    ret = head_rms(ret).reshape(B_, S, RET_VW).astype(h.dtype) * jax.nn.silu(rg)
    aq = rms_norm(aq.reshape(B_, S, ATT_HEADS, ATT_DIM), q_norm_g)
    ak = rms_norm(ak.reshape(B_, S, ATT_HEADS, ATT_DIM), k_norm_g)
    att = chunk_attention(aq, ak, av.reshape(B_, S, ATT_HEADS, ATT_DIM), rel_bias)
    att = att.reshape(B_, S, ATT_W)
    return jnp.concatenate([ret, att], axis=-1) @ w_out

def odd_mixer(h, w_in, w_out):
    B_, S, _ = h.shape
    q, k, v = jnp.split(h @ w_in, 3, axis=-1)
    shp = (B_, S, SB_HEADS, SB_DIM)
    o = stick_breaking(q.reshape(shp), k.reshape(shp), v.reshape(shp))
    return o.reshape(B_, S, SB_W) @ w_out

def grouped_moe(h, router_w, router_b, w_gate, w_up, w_down):
    B_, S, D = h.shape
    t = h.reshape(B_ * S, D)
    scores = jax.nn.sigmoid((t @ router_w).astype(jnp.float32))
    sel = scores + router_b.astype(jnp.float32)
    per_group = N_EXPERTS // N_GROUPS
    group_score = lax.top_k(sel.reshape(-1, N_GROUPS, per_group), TOP_K)[0].sum(-1)
    best_group = jnp.argmax(group_score, axis=-1)
    in_group = (jnp.arange(N_EXPERTS) // per_group)[None, :] == best_group[:, None]
    _, top_idx = lax.top_k(jnp.where(in_group, sel, -jnp.inf), TOP_K)
    top_s = jnp.take_along_axis(scores, top_idx, axis=-1)
    top_w = top_s / jnp.sum(top_s, axis=-1, keepdims=True)
    combine = jnp.einsum('nk,nke->ne', top_w, jax.nn.one_hot(top_idx, N_EXPERTS, dtype=jnp.float32))
    y = jnp.zeros((t.shape[0], D), jnp.float32)
    for e in range(N_EXPERTS):
        he = jax.nn.silu(t @ w_gate[e]) * (t @ w_up[e])
        y = y + combine[:, e:e + 1] * (he @ w_down[e]).astype(jnp.float32)
    return y.reshape(B_, S, D).astype(h.dtype)

def first_inputs(seed: int = 0) -> dict:
    key = jax.random.key(seed)
    ks = jax.random.split(key, 20)

    def nrm(k, shape, s):
        return jax.random.normal(k, shape, jnp.float32) * s

    return {
        "x": nrm(ks[0], (BATCH, SEQ, D_MODEL), 1.0),
        "c": nrm(ks[1], (BATCH, D_MODEL), 1.0),
        "ada_w": nrm(ks[2], (DEPTH, D_MODEL, 6 * D_MODEL), 0.5 * D_MODEL ** -0.5),
        "ada_b": nrm(ks[3], (DEPTH, 6 * D_MODEL), 0.02),
        "norm1_g": 1.0 + nrm(ks[4], (DEPTH, D_MODEL), 0.02),
        "norm2_g": 1.0 + nrm(ks[5], (DEPTH, D_MODEL), 0.02),
        "even_w_in": nrm(ks[6], (N_EVEN, D_MODEL, EVEN_IN), D_MODEL ** -0.5),
        "even_w_out": nrm(ks[7], (N_EVEN, EVEN_MIX, D_MODEL), EVEN_MIX ** -0.5),
        "att_q_norm_g": 1.0 + nrm(ks[8], (N_EVEN, ATT_DIM), 0.02),
        "att_k_norm_g": 1.0 + nrm(ks[9], (N_EVEN, ATT_DIM), 0.02),
        "att_rel_bias": nrm(ks[10], (N_EVEN, ATT_HEADS, REL_SIZE), 0.2),
        "odd_w_in": nrm(ks[11], (N_ODD, D_MODEL, ODD_IN), D_MODEL ** -0.5),
        "odd_w_out": nrm(ks[12], (N_ODD, SB_W, D_MODEL), SB_W ** -0.5),
        "router_w": nrm(ks[13], (D_MODEL, N_EXPERTS), D_MODEL ** -0.5),
        "router_b": nrm(ks[14], (N_EXPERTS,), 0.01),
        "exp_w_gate": nrm(ks[15], (DEPTH, N_EXPERTS, D_MODEL, D_EXPERT), D_MODEL ** -0.5),
        "exp_w_up": nrm(ks[16], (DEPTH, N_EXPERTS, D_MODEL, D_EXPERT), D_MODEL ** -0.5),
        "exp_w_down": nrm(ks[17], (DEPTH, N_EXPERTS, D_EXPERT, D_MODEL), D_EXPERT ** -0.5),
    }

def first_block(x, c, ada_w, ada_b, norm1_g, norm2_g, even_w_in, even_w_out,
              att_q_norm_g, att_k_norm_g, att_rel_bias, odd_w_in, odd_w_out,
              router_w, router_b, exp_w_gate, exp_w_up, exp_w_down):
    S = x.shape[1]
    pos = jnp.arange(S, dtype=jnp.int32)
    c_act = jax.nn.silu(c)
    for layer in range(DEPTH):
        mod = (c_act @ ada_w[layer] + ada_b[layer])[:, None, :]
        sh1, sc1, g1, sh2, sc2, g2 = jnp.split(mod, 6, axis=-1)
        h = rms_norm(x, norm1_g[layer]) * (1.0 + sc1) + sh1
        i = layer // 2
        if layer % 2 == 0:
            mix = even_mixer(h, even_w_in[i], even_w_out[i], att_q_norm_g[i],
                             att_k_norm_g[i], att_rel_bias[i], pos)
        else:
            mix = odd_mixer(h, odd_w_in[i], odd_w_out[i])
        x = x + g1 * mix
        h = rms_norm(x, norm2_g[layer]) * (1.0 + sc2) + sh2
        x = x + g2 * grouped_moe(h, router_w, router_b, exp_w_gate[layer],
                                 exp_w_up[layer], exp_w_down[layer])
    return x


HEAD_DIM = 64
ROPE_DIM = HEAD_DIM // 4
ROPE_THETA = 500000.0
Q_BLOCK = 128
FOX_HEADS = D_MODEL // (2 * HEAD_DIM)
NSA_HEADS = D_MODEL // (2 * HEAD_DIM)
NSA_KV_GROUPS = 2
NSA_HPG = NSA_HEADS // NSA_KV_GROUPS
CMP_BLOCK = 32
CMP_STRIDE = 16
CMP_HIDDEN = 2 * HEAD_DIM
SLC_BLOCK = 64
SLC_TOPK = 16
WINDOW = 512
DIFF_HEADS = D_MODEL // (2 * HEAD_DIM)
MEM_TOKENS = 256
MEM_HEADS = 4
D_FF = 256 * math.ceil(8 * D_MODEL / 3 / 256)
N_EVEN_2 = (DEPTH + 1) // 2
N_ODD_2 = DEPTH // 2
RMS_EPS = 1e-6

FOX_W = FOX_HEADS * HEAD_DIM
NSA_W = NSA_HEADS * HEAD_DIM
NSA_KV_W = NSA_KV_GROUPS * HEAD_DIM
EVEN_SPLITS_2 = (FOX_W, FOX_W, FOX_W, FOX_HEADS, NSA_W) + (NSA_KV_W,) * 6 + (3 * NSA_HEADS,)
EVEN_IN_2 = sum(EVEN_SPLITS_2)
MIX_W = FOX_W + NSA_W
DIFF_QK_W = DIFF_HEADS * 2 * HEAD_DIM
DIFF_V_W = DIFF_HEADS * 2 * HEAD_DIM
ODD_IN_2 = 2 * DIFF_QK_W + DIFF_V_W
MEM_W = MEM_HEADS * HEAD_DIM


def rms_norm_2(x, g):
    xf = x.astype(jnp.float32)
    y = xf * lax.rsqrt(jnp.mean(xf * xf, axis=-1, keepdims=True) + RMS_EPS)
    return (y * g.astype(jnp.float32)).astype(x.dtype)

def rope_tables(positions):
    inv = ROPE_THETA ** (-jnp.arange(0, ROPE_DIM, 2, dtype=jnp.float32) / ROPE_DIM)
    ang = positions.astype(jnp.float32)[..., None] * inv
    return jnp.cos(ang), jnp.sin(ang)

def apply_partial_rope(x, cos, sin):
    half = ROPE_DIM // 2
    x1, x2, rest = x[..., :half], x[..., half:ROPE_DIM], x[..., ROPE_DIM:]
    c = cos[:, :, None, :].astype(x.dtype)
    s = sin[:, :, None, :].astype(x.dtype)
    return jnp.concatenate([x1 * c - x2 * s, x2 * c + x1 * s, rest], axis=-1)

def masked_softmax(logits, mask):
    z = jnp.where(mask, logits.astype(jnp.float32), -jnp.inf)
    m = jnp.max(z, axis=-1, keepdims=True)
    m = jnp.where(jnp.isfinite(m), m, 0.0)
    p = jnp.exp(z - m)
    return p / jnp.maximum(jnp.sum(p, axis=-1, keepdims=True), 1e-30)

def stack_blocks(out, B, T):
    return jnp.moveaxis(out, 0, 1).reshape((B, T) + out.shape[3:])

def fox_attention(q, k, v, log_f):
    B, T, H, dh = q.shape
    c = jnp.cumsum(log_f, axis=1)
    c_k = jnp.transpose(c, (0, 2, 1))[:, :, None, :]
    kpos = jnp.arange(T)
    scale = dh ** -0.5

    def block(i):
        q0 = i * Q_BLOCK
        qb = lax.dynamic_slice_in_dim(q, q0, Q_BLOCK, 1)
        cq = jnp.transpose(lax.dynamic_slice_in_dim(c, q0, Q_BLOCK, 1), (0, 2, 1))[..., None]
        s = jnp.einsum('bqhd,bkhd->bhqk', qb, k).astype(jnp.float32) * scale + (cq - c_k)
        qpos = q0 + jnp.arange(Q_BLOCK)
        p = masked_softmax(s, kpos[None, :] <= qpos[:, None])
        return jnp.einsum('bhqk,bkhd->bqhd', p.astype(v.dtype), v)

    return stack_blocks(lax.map(block, jnp.arange(T // Q_BLOCK)), B, T)

def compress(x, pos, w1, w2):
    B, T, G, dh = x.shape
    nc = (T - CMP_BLOCK) // CMP_STRIDE + 1
    idx = np.arange(nc)[:, None] * CMP_STRIDE + np.arange(CMP_BLOCK)[None, :]
    blocks = x[:, idx] + pos[None, None, :, None, :].astype(x.dtype)
    flat = jnp.moveaxis(blocks, 3, 2).reshape(B, nc, G, CMP_BLOCK * dh)
    return jax.nn.gelu(flat @ w1) @ w2

def nsa_attention(q, kc, vc, ks, vs, kw, vw, gates):
    B, T, H, dh = q.shape
    G = NSA_KV_GROUPS
    nc = kc.shape[1]
    ns = T // SLC_BLOCK
    n_sel = min(SLC_TOPK, ns)
    scale = dh ** -0.5
    cmp_start = np.arange(nc) * CMP_STRIDE
    slc_start = np.arange(ns) * SLC_BLOCK
    cmp_end = jnp.asarray(cmp_start + CMP_BLOCK - 1)
    ov = np.clip(np.minimum(cmp_start[:, None] + CMP_BLOCK, slc_start[None, :] + SLC_BLOCK)
                 - np.maximum(cmp_start[:, None], slc_start[None, :]), 0, None) / CMP_BLOCK
    overlap = jnp.asarray(ov, dtype=jnp.float32)
    blk = jnp.arange(ns)
    k_blocks = jnp.transpose(ks.reshape(B, ns, SLC_BLOCK, G, dh), (0, 3, 1, 2, 4))
    v_blocks = jnp.transpose(vs.reshape(B, ns, SLC_BLOCK, G, dh), (0, 3, 1, 2, 4))
    kw_pad = jnp.pad(kw, ((0, 0), (WINDOW, 0), (0, 0), (0, 0)))
    vw_pad = jnp.pad(vw, ((0, 0), (WINDOW, 0), (0, 0), (0, 0)))
    bi = jnp.arange(B)[:, None, None, None]
    gi = jnp.arange(G)[None, :, None, None]

    def block(i):
        q0 = i * Q_BLOCK
        qpos = q0 + jnp.arange(Q_BLOCK)
        qg = lax.dynamic_slice_in_dim(q, q0, Q_BLOCK, 1).reshape(B, Q_BLOCK, G, NSA_HPG, dh)
        gb = lax.dynamic_slice_in_dim(gates, q0, Q_BLOCK, 1).reshape(B, Q_BLOCK, G, NSA_HPG, 3)
        s_c = jnp.einsum('bqgnd,bcgd->bgnqc', qg, kc).astype(jnp.float32) * scale
        p_c = masked_softmax(s_c, cmp_end[None, :] <= qpos[:, None])
        o_c = jnp.einsum('bgnqc,bcgd->bqgnd', p_c.astype(vc.dtype), vc)
        imp = jnp.einsum('bgnqc,cs->bgqs', p_c, overlap)
        cur = (qpos // SLC_BLOCK)[:, None]
        valid = blk[None, :] * SLC_BLOCK <= qpos[:, None]
        forced = (blk[None, :] == 0) | (blk[None, :] == cur) | (blk[None, :] == cur - 1)
        score = jnp.where(valid, jnp.where(forced, jnp.inf, imp), -jnp.inf)
        _, sel = lax.top_k(score, n_sel)
        k_sel = k_blocks[bi, gi, sel]
        v_sel = v_blocks[bi, gi, sel].reshape(B, G, Q_BLOCK, n_sel * SLC_BLOCK, dh)
        tok = sel[..., None] * SLC_BLOCK + jnp.arange(SLC_BLOCK)
        smask = (tok <= qpos[None, None, :, None, None]).reshape(B, G, 1, Q_BLOCK, n_sel * SLC_BLOCK)
        s_s = jnp.einsum('bqgnd,bgqkld->bgnqkl', qg, k_sel).astype(jnp.float32) * scale
        p_s = masked_softmax(s_s.reshape(B, G, NSA_HPG, Q_BLOCK, n_sel * SLC_BLOCK), smask)
        o_s = jnp.einsum('bgnqm,bgqmd->bqgnd', p_s.astype(v_sel.dtype), v_sel)
        kwb = lax.dynamic_slice_in_dim(kw_pad, q0, WINDOW + Q_BLOCK, 1)
        vwb = lax.dynamic_slice_in_dim(vw_pad, q0, WINDOW + Q_BLOCK, 1)
        kpos = q0 - WINDOW + jnp.arange(WINDOW + Q_BLOCK)
        wmask = ((kpos[None, :] <= qpos[:, None]) & (kpos[None, :] > qpos[:, None] - WINDOW)
                 & (kpos[None, :] >= 0))
        s_w = jnp.einsum('bqgnd,bkgd->bgnqk', qg, kwb).astype(jnp.float32) * scale
        p_w = masked_softmax(s_w, wmask)
        o_w = jnp.einsum('bgnqk,bkgd->bqgnd', p_w.astype(vwb.dtype), vwb)
        o = gb[..., 0:1] * o_c + gb[..., 1:2] * o_s + gb[..., 2:3] * o_w
        return o.reshape(B, Q_BLOCK, H, dh)

    return stack_blocks(lax.map(block, jnp.arange(T // Q_BLOCK)), B, T)

def diff_attention(q1, q2, k1, k2, v, lam):
    B, T, H, dh = q1.shape
    kpos = jnp.arange(T)
    scale = dh ** -0.5

    def block(i):
        q0 = i * Q_BLOCK
        qpos = q0 + jnp.arange(Q_BLOCK)
        mask = kpos[None, :] <= qpos[:, None]
        qb1 = lax.dynamic_slice_in_dim(q1, q0, Q_BLOCK, 1)
        qb2 = lax.dynamic_slice_in_dim(q2, q0, Q_BLOCK, 1)
        a1 = masked_softmax(jnp.einsum('bqhd,bkhd->bhqk', qb1, k1).astype(jnp.float32) * scale, mask)
        a2 = masked_softmax(jnp.einsum('bqhd,bkhd->bhqk', qb2, k2).astype(jnp.float32) * scale, mask)
        p = a1 - lam * a2
        return jnp.einsum('bhqk,bkhd->bqhd', p.astype(v.dtype), v)

    return stack_blocks(lax.map(block, jnp.arange(T // Q_BLOCK)), B, T)

def even_mixer_2(h, cos, sin, w_in, f_bias, cpk, c1k, c2k, cpv, c1v, c2v, w_out):
    B, T, _ = h.shape
    G = NSA_KV_GROUPS
    offsets = [int(o) for o in np.cumsum(EVEN_SPLITS_2)[:-1]]
    fq, fk, fv, fl, nq, kc, vc, ksl, vsl, kwn, vwn, gl = jnp.split(h @ w_in, offsets, axis=-1)
    heads = lambda t, n: t.reshape(B, T, n, HEAD_DIM)
    rope = lambda t: apply_partial_rope(t, cos, sin)
    log_f = jax.nn.log_sigmoid(fl.astype(jnp.float32) + f_bias.astype(jnp.float32))
    o_fox = fox_attention(heads(fq, FOX_HEADS), heads(fk, FOX_HEADS), heads(fv, FOX_HEADS), log_f)
    o_nsa = nsa_attention(
        rope(heads(nq, NSA_HEADS)),
        compress(rope(heads(kc, G)), cpk, c1k, c2k),
        compress(heads(vc, G), cpv, c1v, c2v),
        rope(heads(ksl, G)), heads(vsl, G),
        rope(heads(kwn, G)), heads(vwn, G),
        jax.nn.sigmoid(gl).reshape(B, T, NSA_HEADS, 3))
    o = jnp.concatenate([o_fox.reshape(B, T, FOX_W), o_nsa.reshape(B, T, NSA_W)], axis=-1)
    return o @ w_out

def diff_mixer(h, cos, sin, w_in, lam_p, subln_g, w_out, layer):
    B, T, _ = h.shape
    q, k, v = jnp.split(h @ w_in, [DIFF_QK_W, 2 * DIFF_QK_W], axis=-1)
    q = apply_partial_rope(q.reshape(B, T, 2 * DIFF_HEADS, HEAD_DIM), cos, sin).reshape(B, T, DIFF_HEADS, 2, HEAD_DIM)
    k = apply_partial_rope(k.reshape(B, T, 2 * DIFF_HEADS, HEAD_DIM), cos, sin).reshape(B, T, DIFF_HEADS, 2, HEAD_DIM)
    v = v.reshape(B, T, DIFF_HEADS, 2 * HEAD_DIM)
    lam_init = 0.8 - 0.6 * math.exp(-0.3 * layer)
    lp = lam_p.astype(jnp.float32)
    lam = jnp.exp(jnp.sum(lp[0] * lp[1])) - jnp.exp(jnp.sum(lp[2] * lp[3])) + lam_init
    o = diff_attention(q[..., 0, :], q[..., 1, :], k[..., 0, :], k[..., 1, :], v, lam)
    o = rms_norm_2(o, subln_g) * (1.0 - lam_init)
    return o.reshape(B, T, DIFF_V_W) @ w_out

def memory_cross_attention(h, mem_n, wq, wk, wv, wo):
    B, T, _ = h.shape
    M = mem_n.shape[1]
    q = (h @ wq).reshape(B, T, MEM_HEADS, HEAD_DIM)
    k = (mem_n @ wk).reshape(B, M, MEM_HEADS, HEAD_DIM)
    v = (mem_n @ wv).reshape(B, M, MEM_HEADS, HEAD_DIM)
    s = jnp.einsum('bqhd,bmhd->bhqm', q, k).astype(jnp.float32) * HEAD_DIM ** -0.5
    p = jax.nn.softmax(s, axis=-1)
    o = jnp.einsum('bhqm,bmhd->bqhd', p.astype(v.dtype), v).reshape(B, T, MEM_W)
    return o @ wo

def swiglu(h, wg, wu, wd):
    return (jax.nn.silu(h @ wg) * (h @ wu)) @ wd

def second_inputs(seed: int = 0) -> dict:
    key = jax.random.key(seed)
    ks = jax.random.split(key, 32)

    def nrm(k, shape, fan_in):
        return jax.random.normal(k, shape, jnp.float32) * (fan_in ** -0.5)

    def gain(k, shape):
        return 1.0 + 0.02 * jax.random.normal(k, shape, jnp.float32)

    D = D_MODEL
    flat_cmp = CMP_BLOCK * HEAD_DIM
    return {
        'x': jax.random.normal(ks[0], (BATCH, SEQ, D), jnp.float32),
        'mem': jax.random.normal(ks[1], (BATCH, MEM_TOKENS, D), jnp.float32),
        'positions': jnp.broadcast_to(jnp.arange(SEQ, dtype=jnp.int32), (BATCH, SEQ)),
        'sandwich_g': gain(ks[2], (DEPTH, 6, D)),
        'mem_norm_g': gain(ks[3], (DEPTH, D)),
        'ev_w_in': nrm(ks[4], (N_EVEN_2, D, EVEN_IN_2), D),
        'ev_fox_fbias': 4.0 + 0.5 * jax.random.normal(ks[5], (N_EVEN_2, FOX_HEADS), jnp.float32),
        'ev_cmp_pos_k': 0.02 * jax.random.normal(ks[6], (N_EVEN_2, CMP_BLOCK, HEAD_DIM), jnp.float32),
        'ev_cmp_w1_k': nrm(ks[7], (N_EVEN_2, flat_cmp, CMP_HIDDEN), flat_cmp),
        'ev_cmp_w2_k': nrm(ks[8], (N_EVEN_2, CMP_HIDDEN, HEAD_DIM), CMP_HIDDEN),
        'ev_cmp_pos_v': 0.02 * jax.random.normal(ks[9], (N_EVEN_2, CMP_BLOCK, HEAD_DIM), jnp.float32),
        'ev_cmp_w1_v': nrm(ks[10], (N_EVEN_2, flat_cmp, CMP_HIDDEN), flat_cmp),
        'ev_cmp_w2_v': nrm(ks[11], (N_EVEN_2, CMP_HIDDEN, HEAD_DIM), CMP_HIDDEN),
        'ev_w_out': nrm(ks[12], (N_EVEN_2, MIX_W, D), MIX_W),
        'od_w_in': nrm(ks[13], (N_ODD_2, D, ODD_IN_2), D),
        'od_lambda': 0.1 * jax.random.normal(ks[14], (N_ODD_2, 4, HEAD_DIM), jnp.float32),
        'od_subln_g': gain(ks[15], (N_ODD_2, 2 * HEAD_DIM)),
        'od_w_out': nrm(ks[16], (N_ODD_2, DIFF_V_W, D), DIFF_V_W),
        'ca_wq': nrm(ks[17], (DEPTH, D, MEM_W), D),
        'ca_wk': nrm(ks[18], (DEPTH, D, MEM_W), D),
        'ca_wv': nrm(ks[19], (DEPTH, D, MEM_W), D),
        'ca_wo': nrm(ks[20], (DEPTH, MEM_W, D), MEM_W),
        'ffn_wg': nrm(ks[21], (DEPTH, D, D_FF), D),
        'ffn_wu': nrm(ks[22], (DEPTH, D, D_FF), D),
        'ffn_wd': nrm(ks[23], (DEPTH, D_FF, D), D_FF),
    }

def second_block(x, mem, positions, sandwich_g, mem_norm_g, ev_w_in, ev_fox_fbias,
              ev_cmp_pos_k, ev_cmp_w1_k, ev_cmp_w2_k, ev_cmp_pos_v, ev_cmp_w1_v, ev_cmp_w2_v,
              ev_w_out, od_w_in, od_lambda, od_subln_g, od_w_out,
              ca_wq, ca_wk, ca_wv, ca_wo, ffn_wg, ffn_wu, ffn_wd):
    cos, sin = rope_tables(positions)
    for layer in range(DEPTH):
        g = sandwich_g[layer]
        h = rms_norm_2(x, g[0])
        if layer % 2 == 0:
            e = layer // 2
            y = even_mixer_2(h, cos, sin, ev_w_in[e], ev_fox_fbias[e],
                           ev_cmp_pos_k[e], ev_cmp_w1_k[e], ev_cmp_w2_k[e],
                           ev_cmp_pos_v[e], ev_cmp_w1_v[e], ev_cmp_w2_v[e], ev_w_out[e])
        else:
            o = layer // 2
            y = diff_mixer(h, cos, sin, od_w_in[o], od_lambda[o], od_subln_g[o], od_w_out[o], layer)
        x = x + rms_norm_2(y, g[1])
        mem_n = rms_norm_2(mem, mem_norm_g[layer])
        y = memory_cross_attention(rms_norm_2(x, g[2]), mem_n, ca_wq[layer], ca_wk[layer], ca_wv[layer], ca_wo[layer])
        x = x + rms_norm_2(y, g[3])
        y = swiglu(rms_norm_2(x, g[4]), ffn_wg[layer], ffn_wu[layer], ffn_wd[layer])
        x = x + rms_norm_2(y, g[5])
    return x


def setup_inputs(seed=0):
    out = dict(first_inputs(seed))
    for name, value in second_inputs(seed + 1).items():
        if name != "x":
            out[name + "_2"] = value
    return out


def reference(
    x, c, ada_w, ada_b, norm1_g, norm2_g, even_w_in, even_w_out, att_q_norm_g, att_k_norm_g,
    att_rel_bias, odd_w_in, odd_w_out, router_w, router_b, exp_w_gate, exp_w_up, exp_w_down,
    mem_2, positions_2, sandwich_g_2, mem_norm_g_2, ev_w_in_2, ev_fox_fbias_2, ev_cmp_pos_k_2,
    ev_cmp_w1_k_2, ev_cmp_w2_k_2, ev_cmp_pos_v_2, ev_cmp_w1_v_2, ev_cmp_w2_v_2, ev_w_out_2,
    od_w_in_2, od_lambda_2, od_subln_g_2, od_w_out_2, ca_wq_2, ca_wk_2, ca_wv_2, ca_wo_2,
    ffn_wg_2, ffn_wu_2, ffn_wd_2,
):
    x = first_block(
        x, c, ada_w, ada_b, norm1_g, norm2_g, even_w_in, even_w_out, att_q_norm_g, att_k_norm_g,
        att_rel_bias, odd_w_in, odd_w_out, router_w, router_b, exp_w_gate, exp_w_up, exp_w_down,
    )
    return second_block(
        x, mem_2, positions_2, sandwich_g_2, mem_norm_g_2, ev_w_in_2, ev_fox_fbias_2,
        ev_cmp_pos_k_2, ev_cmp_w1_k_2, ev_cmp_w2_k_2, ev_cmp_pos_v_2, ev_cmp_w1_v_2,
        ev_cmp_w2_v_2, ev_w_out_2, od_w_in_2, od_lambda_2, od_subln_g_2, od_w_out_2, ca_wq_2,
        ca_wk_2, ca_wv_2, ca_wo_2, ffn_wg_2, ffn_wu_2, ffn_wd_2,
    )


_drawn_inputs = setup_inputs


def setup_inputs(seed=0):
    import zlib

    import numpy as np

    out = dict(_drawn_inputs(seed))
    spreads = {}
    factors = {'att_q_norm_g': 8.0,
     'att_k_norm_g': 3.837,
     'ev_cmp_pos_k_2': 29.431,
     'ev_cmp_pos_v_2': 4.089,
     'od_lambda_2': 8.0,
     'od_subln_g_2': 64.0,
     'att_rel_bias': 3.241}
    for name, (base, spread) in spreads.items():
        noise = np.random.default_rng([zlib.crc32(name.encode()), seed]).standard_normal(out[name].shape)
        drawn = base * np.exp(spread * noise) if base else spread * noise
        out[name] = __import__('jax').numpy.asarray(drawn.astype(out[name].dtype))
    for name, factor in factors.items():
        out[name] = (out[name] * factor).astype(out[name].dtype)
    return out
```

```python
import concourse.bass as bass
from concourse import mybir
from contextlib import ExitStack
import numpy as np

F32 = mybir.dt.float32
I32 = mybir.dt.int32
ALU = mybir.AluOpType
ACT = mybir.ActivationFunctionType
AX = mybir.AxisListType

S, D = 256, 1024
TB = S // 128
KD = D // 128
CHUNK = 64
RET_HEADS, RET_DIM = 4, 128
ATT_HEADS = 8
HD = 64
EXPERTS, GROUPS, PER_GROUP, D_EXP = 16, 4, 4, 512
D_FF = 2816
EVEN_IN, ODD_IN, EV_IN, OD_IN = 3584, 3072, 2848, 3072
MEM_HEADS, MEM_W = 4, 256
CMP_N = 15
SLOTS = 128
RING = 4
TILE = 4096
NEG = -1.0e30
EPS = 1e-6
FFN_STEP = 256
FFN_STEPS = D_FF // FFN_STEP
PASSES = GROUPS
PASS_TILES = 3 * PER_GROUP


class Count:

    def __init__(self, sem, at=0):
        self.sem, self.at, self.n = sem, at, 0

    def up(self):
        self.n += 1
        return self.sem, 1

    def now(self):
        return self.sem, self.at + self.n


class Plan:

    def __init__(self):
        self.tiles, self.chunks, self.turns = [], [], {}
        self.pe_tiles = self.halves = 0
        self.evac = {"act": 0, "dve": 0}
        self.n_turns = 0
        self.loads = [0] * RING

    def tile(self, name, dmas=1, user="pe"):
        n = len(self.tiles)
        self.loads[n % RING] += 16 * dmas
        order = None
        if user == "pe":
            order, self.pe_tiles = self.pe_tiles, self.pe_tiles + 1
        self.tiles.append(dict(name=name, n=n, slot=n % RING, loaded=self.loads[n % RING], user=user, order=order))
        return n

    def chunk(self, tile, last, evac):
        if last:
            ready = ("weights_used", self.tiles[tile]["order"] + 1)
        else:
            self.halves += 1
            ready = ("chunk_ready", self.halves)
        self.evac[evac] += 1
        self.chunks.append(dict(q=len(self.chunks), tile=tile, ready=ready, evac=evac, done=self.evac[evac]))
        return len(self.chunks) - 1

    def turn(self, name, items):
        self.turns[name] = (self.n_turns, items)
        self.n_turns += items


def make_plan():
    p = Plan()
    st = {}

    def proj(name, cols, evac):
        out = []
        for j in range(-(-cols // 512)):
            t = p.tile(f"{name}{j}")
            out.append((t, [p.chunk(t, tb == 1, evac) for tb in range(TB)]))
        st[name] = out

    def experts(l):
        first = len(p.tiles)
        for g in range(PASSES):
            for k in ["g0", "u0", "g1", "u1", "d0", "g2", "u2", "d1", "g3", "u3", "d2", "d3"]:
                p.tile(f"moe{l}.{g}.{k}")
        st[f"moe{l}"] = first

    def feed_forward(l):
        first = p.tile(f"ffn{l}.gu0", 2)
        for s in range(1, FFN_STEPS):
            p.tile(f"ffn{l}.gu{s}", 2)
            p.tile(f"ffn{l}.dn{s-1}")
        p.tile(f"ffn{l}.dn{FFN_STEPS-1}")
        st[f"ffn{l}"] = first

    def cross(l):
        t = p.tile(f"qo{l}", 2)
        st[f"caq{l}"] = (t, [p.chunk(t, False, "act") for _ in range(2)])
        st[f"cao{l}"] = (t, [p.chunk(t, i == 3, "act") for i in range(4)])

    for l in range(2):
        p.turn(f"mem{l}", KD)
        t = p.tile(f"kv{l}", 2)
        st[f"kv{l}"] = (t, [p.chunk(t, i == 3, "act") for i in range(4)])
    st["ada0"] = [p.tile(f"ada0.{j}", 1, "dve") for j in range(12)]
    p.turn("a0h1", KD)
    st["ada1"], st["even_in"] = [], []
    for j in range(7):
        if j < 6:
            st["ada1"] += [p.tile(f"ada1.{2*j+i}", 1, "dve") for i in range(2)]
        t = p.tile(f"even_in{j}")
        st["even_in"].append((t, [p.chunk(t, tb == 1, "act") for tb in range(TB)]))
    p.turn("a0ret", 8)
    p.turn("a0att", 8)
    p.turn("a0mix", KD)
    proj("even_out", D, "dve")
    p.turn("a0h2", KD)
    experts(0)
    p.turn("a1h1", KD)
    proj("odd_in", ODD_IN, "act")
    p.turn("a1qk", 16)
    proj("odd_out", D, "dve")
    p.turn("a1h2", KD)
    experts(1)
    p.turn("b0h0", KD)
    proj("ev_in", EV_IN, "act")
    p.turn("b0qk", 16)
    st["cmp"] = p.tile("cmp", 2)
    p.turn("b0mix", KD)
    proj("ev_out", D, "act")
    p.turn("b0h2", KD)
    cross(0)
    p.turn("b0ca", 2)
    p.turn("b0h4", KD)
    feed_forward(0)
    p.turn("b1h0", KD)
    proj("od_in", OD_IN, "act")
    p.turn("b1qk", 16)
    p.turn("b1mix", KD)
    proj("od_out", D, "act")
    p.turn("b1h2", KD)
    cross(1)
    p.turn("b1ca", 2)
    p.turn("b1h4", KD)
    feed_forward(1)
    return p, st


def build(nc, a, out):
    plan, st = make_plan()
    tiles, chunks, turns = plan.tiles, plan.chunks, plan.turns
    ctx = ExitStack()
    with ctx:
        def sb(name, shape, dt=F32):
            return ctx.enter_context(nc.sbuf_tensor(name, shape, dt))

        def sem(name):
            return ctx.enter_context(nc.semaphore(name))

        W = sb("weight_ring", [128, RING, TILE])
        X = sb("x_state", [128, TB, D])
        NB = sb("normed", [128, TB, D])
        HT = sb("features", [128, KD, S])
        PR = sb("projected", [128, TB * EVEN_IN])
        QK = sb("qk_features", [128, 16, S])
        AUX = sb("aux", [128, 5120])
        GB = sb("row_gains", [128, 4, D])
        MK = sb("mem_keys", [128, 2, 2, S])
        MV = sb("mem_values", [128, 2, TB, MEM_W])
        CS = sb("constants", [128, a["consts"].shape[1]])
        GM = sb("feature_gains", [128, 12, KD])
        MOD = sb("modulation", [128, 2, 48])
        SCL = sb("gain_times_scale", [128, 4, KD])
        ACC = sb("ada_sum", [128, 2, 512])
        ABF = sb("ada_bias_features", [128, 2, 48])
        CF = sb("c_features", [128, KD])
        AG = sb("qk_norm_gains", [128, 3])
        W2 = sb("cmp_w2", [128, 192])
        POS = sb("cmp_positions", [128, 2, 16])
        RW = sb("router_w", [128, KD, EXPERTS])
        RB = sb("router_b", [128, EXPERTS])
        SCR = sb("scratch", [128, 8, 384])
        ST = sb("small", [128, 320])
        VAR = sb("variance", [128, 32])
        ROOT = sb("root", [128, 32])
        RSD = sb("reciprocal_root", [128, 32])
        SS = sb("square_sums", [128, 4])
        KEY = sb("slot_key", [128, TB])
        CMB = sb("combine", [128, TB, PER_GROUP])
        FINI = sb("finisher", [128, 1])
        RC = sb("sum_reciprocals", [128, 8])
        LAM_ = sb("minus_lambda", [128, 1])
        LAM = LAM_[:, :]
        ROPE = sb("rope_cos_sin", [128, 2, TB, 8])
        PI = sb("positions", [128, TB], I32)
        FB = sb("forget_bias", [128, 8])
        FLAG = sb("overflow_flag", [128, 2], I32)
        ident, ones = CS[:, 0:128], CS[:, 256:384]
        before = CS[:, 128:256]
        strict = CS[:, 128:512]
        upto = CS[:, 512:640]
        after = CS[:, 640:768]
        iota = CS[:, 768:896]
        causal = [CS[:, 1152:1280], CS[:, 1024:1280]]
        nomask = CS[:, 896:1152]
        chunk_mask = CS[:, 1280:1664]
        cos_a = CS[:, 1664:1792].rearrange("p (t n) -> p t n", t=TB)
        sin_a = CS[:, 1792:1920].rearrange("p (t n) -> p t n", t=TB)
        block_mask = CS[:, 1920:1928]
        cmp_keep = CS[:, 1928:1960].rearrange("p (t n) -> p t n", t=TB)
        cmp_add = CS[:, 1960:1992].rearrange("p (t n) -> p t n", t=TB)
        inv_freq = CS[:, 1992:2000]
        lower44 = CS[:, 2000:2016].rearrange("p (j i) -> p j i", j=4)
        iota4 = CS[:, 2016:2020]
        decay = AUX[:, 0:1536].rearrange("p (h n) -> p h n", h=RET_HEADS)
        bias = AUX[:, 1536:4608].rearrange("p (h n) -> p h n", h=ATT_HEADS)

        B = [ctx.enter_context(nc.psum_tensor(f"bank{i}", [128, 512], F32)) for i in range(8)]

        def pview(n):
            return PR[:, 0:TB * n].rearrange("p (t n) -> p t n", t=TB)

        w_loaded = [sem(f"weights_loaded{i}") for i in range(RING)]
        weights_used = sem("weights_used")
        chunk_ready = sem("chunk_ready")
        S_ = {"weights_used": weights_used, "chunk_ready": chunk_ready}
        copied = {"act": sem("chunk_taken_by_act"), "dve": sem("chunk_taken_by_dve")}
        ada_summed = sem("ada_summed")
        ada_row_loaded = sem("ada_row_loaded")
        mod_ready = sem("mod_in_psum")
        mod_taken = sem("mod_taken")
        turned = sem("transposed")
        turn_taken = [sem("transposed_taken_by_act"), sem("transposed_taken_by_dve")]
        x_loaded, mem_loaded, consts_loaded = sem("x_loaded"), sem("mem_loaded"), sem("consts_loaded")
        aux_loaded = sem("aux_loaded")
        vec_done, act_done = sem("vec_done"), sem("act_done")
        squares = sem("squares_summed")
        var_ready, root_ready, normed = sem("variance_ready"), sem("root_ready"), sem("normed")
        x_ready = sem("x_ready")
        scores_ready, shifted, probs_ready = sem("scores_ready"), sem("scores_shifted"), sem("probs_ready")
        probs_turned, probs_copied = sem("probs_transposed"), sem("probs_copied")
        values_ready, head_done = sem("weighted_values"), sem("head_done")
        a0_rotated, a0_mixed = sem("a0_rotated"), sem("a0_mixed")
        ret_scores, ret_decayed = sem("retention_scores"), sem("retention_decayed")
        ret_values, ret_out = sem("retention_values"), sem("retention_out")
        stick_scored, stick_z, stick_logs = sem("stick_scored"), sem("stick_z"), sem("stick_logs")
        stick_log, stick_summed, stick_arg = sem("stick_log1p"), sem("stick_summed"), sem("stick_arg")
        stick_exp, stick_probs = sem("stick_exp"), sem("stick_probs")
        stick_valued, stick_out = sem("stick_valued"), sem("stick_out")
        b0_roped, b1_roped, gates_summed = sem("b0_roped"), sem("b1_roped"), sem("gates_summed")
        gates_copied = sem("gates_copied")
        cmp_pe, cmp_act, cmp_dve = sem("compress_pe"), sem("compress_act"), sem("compress_dve")
        probs_joined = sem("probs_joined")
        groups_chosen = sem("groups_chosen")
        scales_ready, gains_loaded, b1_mixed = sem("scales_ready"), sem("gains_loaded"), sem("b1_mixed")
        ask_act, told_act = sem("asked_of_act"), sem("done_by_act")
        plan_ready = sem("routing_ready")
        router_ready = sem("router_products")
        ffn_gate, ffn_up, ffn_silu, ffn_he = sem("ffn_gate"), sem("ffn_up"), sem("ffn_silu"), sem("ffn_hidden")
        out_stored = sem("out_stored")
        NAMES = ["slots_chosen", "gathered", "slot_weights", "back_ready", "feat_act", "feat_dve", "back_copied",
                 "silu", "hidden", "turned", "turned_copied", "y_act", "y_dve", "scattered", "added", "steps",
                 "used"]
        moe = {n: sem("moe_" + n) for n in NAMES[:-1]}
        moe["used"] = weights_used
        ovf = [{n: sem(f"over{l}_" + n) for n in NAMES} for l in range(2)]
        ovf_loaded = [[sem(f"over{l}_loaded{i}") for i in range(RING)] for l in range(2)]

        XG = PR[:, 0:1024].rearrange("p (k n) -> p k n", k=KD)
        SG = [PR[:, 1024 + 512 * i:1536 + 512 * i] for i in range(2)]
        HE = [PR[:, 2048 + 512 * i:2560 + 512 * i] for i in range(2)]
        HET = [PR[:, 3072 + 512 * i:3584 + 512 * i].rearrange("p (k n) -> p k n", k=4) for i in range(2)]
        YE = PR[:, 4096:5120]
        SEL = PR[:, 5120:5376].rearrange("p (t n) -> p t n", t=TB)
        BACK = PR[:, 5376:5632].rearrange("p (t n) -> p t n", t=TB)
        TMP = [PR[:, 5632 + 512 * i:6144 + 512 * i] for i in range(2)]
        WSL = PR[:, 6656:6660]
        FSG = [PR[:, 256 * i:256 * (i + 1)] for i in range(2)]
        FHE = [PR[:, 512 + 256 * i:768 + 256 * i] for i in range(4)]

        def slot(n):
            return W[:, n % RING, :]

        def cols(w, lo, n, k=KD):
            return w.rearrange("(k p) n -> p k n", p=128)[:, :, lo:lo + n]

        PASS_ORDER = [("g", 0), ("u", 0), ("g", 1), ("u", 1), ("d", 0), ("g", 2), ("u", 2), ("d", 1),
                      ("g", 3), ("u", 3), ("d", 2), ("d", 3)]
        PLACE = {x: i for i, x in enumerate(PASS_ORDER)}

        STICKS = 16
        W2K, W2V = W2[:, 0:128], W2[:, 128:192]
        REP = CS[:, 2020:2148]
        CT = AUX[:, 3072:3328]
        VC, VB, KC = AUX[:, 3328:3456], AUX[:, 3456:3968], AUX[:, 3968:3998]
        CP = SCR[:, 0, 0:256].rearrange("p (t n) -> p t n", t=TB)
        PCT = SCR[:, 1, 0:256]
        possel = AUX[:, 0:2048].rearrange("p (h n) -> p h n", h=8)
        negsel = AUX[:, 2048:3072].rearrange("p (h n) -> p h n", h=8)
        GT = ST[:, 264:312].rearrange("p (t n) -> p t n", t=TB)
        Y = AUX[:, 0:2048].rearrange("p (t n) -> p t n", t=TB)

        def units_of(name, P):
            out = []
            heads = {"a0": 8, "b0": 24, "ca0": 4, "ca1": 4, "b1": 8}[name]
            for i in range(heads):
                kind, h = ("fox", i) if i < 8 else ("slc" if i < 16 else "win", i % 8)
                lo = HD * (h % 2)
                rows = slice(lo, lo + HD)
                for tb in range(TB):
                    nk = S if name[:2] == "ca" else 128 * (tb + 1)
                    here = slice(tb * 128, (tb + 1) * 128)
                    d = dict(nk=nk, mask=causal[tb], scale=HD ** -0.5, gate=None, add=False)
                    if name == "a0":
                        d.update(scores=[[(QK[rows, 8 + h // 2, here], QK[rows, 12 + h // 2, 0:nk])]],
                                 mask=bias[:, h, 128 * tb:128 * tb + nk], out=NB[:, tb, 512 + HD * h:512 + HD * (h + 1)],
                                 v=lambda jb, h=h: P[:, jb, 3072 + HD * h:3072 + HD * (h + 1)])
                    elif name[:2] == "ca":
                        l = int(name[2])
                        d.update(scores=[[(QK[rows, h // 2, here], MK[rows, l, h // 2, :])]], mask=nomask,
                                 out=NB[:, tb, HD * h:HD * (h + 1)],
                                 v=lambda jb, h=h, l=l: MV[:, l, jb, HD * h:HD * (h + 1)])
                    elif name == "b1":
                        d.update(scores=[[(QK[HD * s:HD * (s + 1), h, here], QK[HD * s:HD * (s + 1), 8 + h, 0:nk])]
                                         for s in range(2)],
                                 out=NB[:, tb, 128 * h:128 * (h + 1)],
                                 v=lambda jb, h=h: P[:, jb, 2048 + 128 * h:2048 + 128 * (h + 1)])
                    elif kind == "fox":
                        own = slice(lo, lo + 8)
                        d.update(scores=[[(QK[rows, h // 2, here], QK[rows, 4 + h // 2, 0:nk]),
                                          (CT[own, here], possel[own, h, 0:nk]), (negsel[own, h, :], CT[own, 0:nk])]],
                                 out=NB[:, tb, HD * h:HD * (h + 1)],
                                 v=lambda jb, h=h: P[:, jb, 1024 + HD * h:1024 + HD * (h + 1)])
                    else:
                        b = 0 if kind == "slc" else 1
                        at = (2440, 2696)[b] + HD * (h // 4)
                        d.update(scores=[[(QK[rows, 8 + h // 2, here], QK[rows, 12 + 2 * b + h // 4, 0:nk])]],
                                 gate=GT[:, tb, 3 * h + 1 + b:3 * h + 2 + b], add=True,
                                 out=NB[:, tb, 512 + HD * h:512 + HD * (h + 1)],
                                 v=lambda jb, at=at: P[:, jb, at:at + HD])
                    out.append(d)
            return out

        UNITS = {"a0": (0, 16), "b0": (16, 64), "ca0": (64, 72), "b1": (72, 88), "ca1": (88, 96)}
        CONSTS = 16 * 14

        block = ctx.enter_context(nc.Block())

        @block.sync
        def _(eng):
            def free(n):
                if n >= RING:
                    old = tiles[n - RING]
                    if old["user"] == "pe":
                        eng.wait_ge(weights_used, old["order"] + 1)
                    else:
                        eng.wait_ge(ada_summed, old["ordinal"])

            def load(n, parts):
                free(n)
                for dst, src in parts:
                    eng.dma_start(dst, src).then_inc(w_loaded[n % RING], 16)

            def wide(n, w, lo, width=512):
                dst = slot(n)[:, 0:KD * width].rearrange("p (k n) -> p k n", k=KD)
                load(n, [(dst, cols(w, lo, width))])

            def halves(n, wa, wb, ka=KD, kb=KD, na=256, nb=256):
                load(n, [(slot(n)[:, 0:2048].rearrange("p (k n) -> p k n", k=ka), cols(wa, 0, na)),
                         (slot(n)[:, 2048:4096].rearrange("p (k n) -> p k n", k=kb), cols(wb, 0, nb))])

            done = 0
            for j in range(24):
                tiles[(st["ada0"] + st["ada1"])[j]]["ordinal"] = j + 1
            for l in range(2):
                halves(st[f"kv{l}"][0], a["ca_wk_2"][l], a["ca_wv_2"][l])
            for j, n in enumerate(st["ada0"]):
                wide(n, a["ada_w"][0], 512 * j)
            for j in range(7):
                if j < 6:
                    for i in range(2):
                        wide(st["ada1"][2 * j + i], a["ada_w"][1], 512 * (2 * j + i))
                wide(st["even_in"][j][0], a["even_w_in"][0], 512 * j)
            for j in range(2):
                wide(st["even_out"][j][0], a["even_w_out"][0], 512 * j)

            mats = {"g": "exp_w_gate", "u": "exp_w_up", "d": "exp_w_down"}

            def expert_source(l, kind, group, e):
                w = a[mats[kind]][l].rearrange("(g e) (k p) n -> g e p k n", e=PER_GROUP, p=128)
                return w[group, e]

            def expert_slot(n, kind):
                return slot(n).rearrange("p (k n) -> p k n", k=4 if kind == "d" else KD)

            def experts(l):
                base = st[f"moe{l}"]
                with eng.Fori(0, PASSES) as g:
                    for i, (kind, e) in enumerate(PASS_ORDER):
                        t = tiles[base + i]
                        eng.wait_ge(weights_used, tiles[base]["order"] + i - RING + 1 + g * PASS_TILES)
                        eng.dma_start(expert_slot(t["n"], kind), expert_source(l, kind, g, e))\
                            .then_inc(w_loaded[t["slot"]], 16)
                eng.wait_ge(plan_ready, l + 1)
                over = eng.value_load(FLAG[0:1, 0:1], min_val=0, max_val=1)
                group = eng.value_load(FLAG[0:1, 1:2], min_val=0, max_val=GROUPS - 1)
                with eng.If(over == 1):
                    last = tiles[base + PASSES * PASS_TILES - 1]["order"] + 1
                    eng.wait_ge(weights_used, last)
                    for i, (kind, e) in enumerate(PASS_ORDER):
                        if i >= RING:
                            eng.wait_ge(ovf[l]["used"], i - RING + 1)
                        eng.dma_start(expert_slot(i, kind), expert_source(l, kind, group, e))\
                            .then_inc(ovf_loaded[l][i % RING], 16)
                    eng.wait_ge(ovf[l]["used"], PASS_TILES)

            def feed_forward(l):
                base = st[f"ffn{l}"]
                wg, wu, wd = a["ffn_wg_2"][l], a["ffn_wu_2"][l], a["ffn_wd_2"][l]
                gv = wg.rearrange("(k p) (s n) -> s p k n", p=128, n=FFN_STEP)
                uv = wu.rearrange("(k p) (s n) -> s p k n", p=128, n=FFN_STEP)
                dv = wd.rearrange("(s k p) n -> s p k n", p=128, k=2)

                def up_tile(n, s, dyn=None):
                    b = slot(n)
                    for src, at in ((gv, 0), (uv, 2048)):
                        eng.dma_start(b[:, at:at + 2048].rearrange("p (k n) -> p k n", k=KD), src[s])\
                            .then_inc(w_loaded[n % RING], 16)

                def down_tile(n, s):
                    eng.dma_start(slot(n)[:, 0:2048].rearrange("p (k n) -> p k n", k=2), dv[s])\
                        .then_inc(w_loaded[n % RING], 16)

                free(base)
                up_tile(base, 0)
                order = tiles[base]["order"]
                with eng.Fori(0, (FFN_STEPS - 1) // 2) as i:
                    for j in range(4):
                        n = base + 1 + j
                        eng.wait_ge(weights_used, order + 1 + j - RING + 1 + i * 4)
                        if j % 2 == 0:
                            up_tile(n, i * 2 + (1 + j // 2))
                        else:
                            down_tile(n, i * 2 + j // 2)
                n = base + 2 * FFN_STEPS - 1
                free(n)
                down_tile(n, FFN_STEPS - 1)

            def stream(name, w, n):
                for j, (t, _) in enumerate(st[name]):
                    wide(t, w, 512 * j, min(512, n - 512 * j))

            def cross(l):
                halves(tiles_of(f"caq{l}"), a["ca_wq_2"][l], a["ca_wo_2"][l], kb=2, nb=D)

            def tiles_of(name):
                return st[name][0]

            experts(0)
            stream("odd_in", a["odd_w_in"][0], ODD_IN)
            stream("odd_out", a["odd_w_out"][0], D)
            experts(1)
            stream("ev_in", a["ev_w_in_2"][0], EV_IN)
            load(st["cmp"], [(slot(st["cmp"])[:, 2048 * i:2048 * (i + 1)].rearrange("p (k n) -> p k n", k=16),
                              a[w][0].rearrange("(k p) n -> p k n", p=128))
                             for i, w in enumerate(("ev_cmp_w1_k_2", "ev_cmp_w1_v_2"))])
            stream("ev_out", a["ev_w_out_2"][0], D)
            cross(0)
            feed_forward(0)
            stream("od_in", a["od_w_in_2"][0], OD_IN)
            stream("od_out", a["od_w_out_2"][0], D)
            cross(1)
            feed_forward(1)
            eng.wait_ge(x_ready, 10)
            eng.dma_start(out.rearrange("b (t p) d -> p (b t) d", p=128), X[:, :, :]).then_inc(out_stored, 16)
            eng.wait_ge(out_stored, 16)

        @block.tensor
        def _(eng):
            used = Count(weights_used)
            half = Count(chunk_ready)
            trn = Count(turned)
            unit, vunit = [0], [0]

            def loaded(n):
                eng.wait_ge(w_loaded[tiles[n]["slot"]], tiles[n]["loaded"])

            def turn(name, source, parts=128):
                first, items = turns[name]
                for i in range(items):
                    x = first + i
                    if x >= 4:
                        eng.wait_ge(turn_taken[x % 2], (x - 4) // 2 + 1)
                    for tb in range(TB):
                        mm = eng.transpose(B[x % 4][:, tb * 128:(tb + 1) * 128], source(i, tb), ident)
                    mm.then_inc(*trn.up())

            def turns_taken(name):
                first, items = turns[name]
                for e in range(2):
                    eng.wait_ge(turn_taken[e], (first + items) // 2)

            def chunk(q, products):
                c = chunks[q]
                if q >= 2:
                    eng.wait_ge(copied[chunks[q - 2]["evac"]], chunks[q - 2]["done"])
                n = products[0][1].shape[-1]
                for i, (left, right) in enumerate(products):
                    mm = eng.matmul(B[4 + q % 2][:, 0:n], left, right, start=(i == 0), stop=(i == len(products) - 1))
                count = used if c["ready"][0] == "weights_used" else half
                mm.then_inc(*count.up())
                assert count.now()[1] == c["ready"][1]

            def project(name, width=None):
                for j, (t, qs) in enumerate(st[name]):
                    n = 512 if width is None else min(512, width - 512 * j)
                    w = slot(t)[:, 0:KD * n].rearrange("p (k n) -> p k n", k=KD)
                    loaded(t)
                    for tb, q in enumerate(qs):
                        chunk(q, [(HT[:, k, tb * 128:(tb + 1) * 128], w[:, k, :]) for k in range(KD)])

            ada = [0]

            def modulation():
                j = ada[0]
                ada[0] += 1
                eng.wait_ge(ada_summed, j + 1)
                if j >= 2:
                    eng.wait_ge(mod_taken, j - 1)
                bank = B[6 + j % 2]
                if (j % 12) // 2 in (2, 5):
                    mm = eng.matmul(bank[:, :], ones, ACC[:, j % 2, :], start=True, stop=True)
                else:
                    for i in range(4):
                        mm = eng.matmul(bank[:, i:i + 1], ACC[:, j % 2, i * 128:(i + 1) * 128], ones[:, 0:1],
                                        start=True, stop=True)
                mm.then_inc(mod_ready, 1)

            normed_n = [0]

            def turn_normed(name):
                normed_n[0] += 1
                eng.wait_ge(normed, normed_n[0])
                turn(name, lambda i, tb: NB[:, tb, i * 128:(i + 1) * 128])
                turns_taken(name)

            def attention(units):
                n, u0, v0 = len(units), unit[0], vunit[0]
                per = len(units[0]["scores"])
                unit[0] += n * per
                vunit[0] += n
                for t in range(n + 2):
                    if t < n:
                        d = units[t]
                        for j, products in enumerate(d["scores"]):
                            u = u0 + t * per + j
                            if u >= 2:
                                eng.wait_ge(shifted, u - 1)
                            for i, (left, right) in enumerate(products):
                                mm = eng.matmul(B[u % 2][:, 0:d["nk"]], left, right, start=(i == 0),
                                                stop=(i == len(products) - 1))
                            mm.then_inc(scores_ready, 1)
                    if 1 <= t <= n:
                        v, d = v0 + t - 1, units[t - 1]
                        if per == 1:
                            eng.wait_ge(probs_ready, u0 + t)
                            p = SCR[:, 2 + (u0 + t - 1) % 2, :]
                        else:
                            eng.wait_ge(probs_joined, t)
                            p = SCR[:, 6 + (t - 1) % 2, :]
                        if v >= 2:
                            eng.wait_ge(probs_copied, v - 1)
                        for jb in range(d["nk"] // 128):
                            mm = eng.transpose(B[2 + v % 2][:, jb * 128:(jb + 1) * 128],
                                               p[:, jb * 128:(jb + 1) * 128], ident)
                        mm.then_inc(probs_turned, 1)
                    if t >= 2:
                        v, d = v0 + t - 2, units[t - 2]
                        eng.wait_ge(probs_copied, v + 1)
                        if v >= 2:
                            eng.wait_ge(head_done, v - 1)
                        nb = d["nk"] // 128
                        for jb in range(nb):
                            mm = eng.matmul(B[4 + v % 2][:, 0:d["out"].shape[-1]],
                                            SCR[:, 4 + v % 2, jb * 128:(jb + 1) * 128],
                                            d["v"](jb), start=(jb == 0), stop=(jb == nb - 1))
                        mm.then_inc(values_ready, 1)

            def experts_pass(m, P, wait_tile, order):
                def w(kind, e):
                    i = PLACE[kind, e]
                    return wait_tile(i).rearrange("p (k n) -> p k n", k=4 if kind == "d" else KD)

                eng.wait_ge(m["slots_chosen"], P + 1)
                for b in range(2):
                    for k in range(4):
                        for tb in range(TB):
                            mm = eng.matmul(B[b][:, k * 128:(k + 1) * 128],
                                            NB[:, tb, (4 * b + k) * 128:(4 * b + k + 1) * 128], SEL[:, tb, :],
                                            start=(tb == 0), stop=(tb == TB - 1))
                    mm.then_inc(m["gathered"], 1)
                for tb in range(TB):
                    mm = eng.matmul(B[2][:, 0:4], SEL[:, tb, :], CMB[:, tb, :], start=(tb == 0), stop=(tb == TB - 1))
                mm.then_inc(m["slot_weights"], 1)
                for tb in range(TB):
                    mm = eng.transpose(B[3][:, tb * 128:(tb + 1) * 128], SEL[:, tb, :], ident)
                mm.then_inc(m["back_ready"], 1)

                def gate_up(e):
                    if e == 0:
                        eng.wait_ge(m["feat_act"], P + 1)
                        eng.wait_ge(m["feat_dve"], P + 1)
                    if e < 2:
                        eng.wait_ge(m["added"], P * 4 + 1)
                    else:
                        eng.wait_ge(m["hidden"], P * 4 + (e - 1))
                    for i, kind in enumerate("gu"):
                        v = w(kind, e)
                        for k in range(KD):
                            mm = eng.matmul(B[4 + 2 * (e % 2) + i][:, :], XG[:, k, :], v[:, k, :],
                                            start=(k == 0), stop=(k == KD - 1))
                        mm.then_inc(m["used"], 1)

                def turn_hidden(e):
                    eng.wait_ge(m["hidden"], P * 4 + (e + 1))
                    if e == 1:
                        eng.wait_ge(m["back_copied"], P + 1)
                    if e >= 2:
                        eng.wait_ge(m["turned_copied"], P * 4 + (e - 1))
                    for k in range(4):
                        mm = eng.transpose(B[2 + e % 2][:, k * 128:(k + 1) * 128],
                                           HE[e % 2][:, k * 128:(k + 1) * 128], ident)
                    mm.then_inc(m["turned"], 1)

                def down(e):
                    eng.wait_ge(m["turned_copied"], P * 4 + (e + 1))
                    v = w("d", e)
                    for k in range(4):
                        for h in range(2):
                            mm = eng.matmul(B[h][:, :], HET[e % 2][:, k, :], v[:, k, h * 512:(h + 1) * 512],
                                            start=(e == 0 and k == 0), stop=(e == 3 and k == 3),
                                            skip_group_check=True)
                    mm.then_inc(m["used"], 1)

                gate_up(0)
                gate_up(1)
                turn_hidden(0)
                down(0)
                gate_up(2)
                turn_hidden(1)
                down(1)
                gate_up(3)
                turn_hidden(2)
                down(2)
                turn_hidden(3)
                down(3)
                for h in range(2):
                    eng.wait_ge(m["y_dve" if h else "y_act"], P + 1)
                    for tb in range(TB):
                        eng.matmul(B[4 + 2 * h + tb][:, :], BACK[:, tb, :], YE[:, h * 512:(h + 1) * 512],
                                   start=True, stop=True).then_inc(m["scattered"], 1)

            def route(l):
                for tb in range(TB):
                    for k in range(KD):
                        mm = eng.matmul(B[6][:, tb * 16:(tb + 1) * 16], HT[:, k, tb * 128:(tb + 1) * 128], RW[:, k, :],
                                        start=(k == 0), stop=(k == KD - 1))
                mm.then_inc(router_ready, 1)
                hot = ST[:, 256:264].rearrange("p (t g) -> p t g", t=TB)
                eng.wait_ge(groups_chosen, l + 1)
                eng.matmul(B[7][:, 0:4], before, hot[:, 0, :], start=True, stop=True)
                eng.matmul(B[7][:, 4:8], ones, hot[:, 0, :], start=True, stop=False)
                eng.matmul(B[7][:, 4:8], before, hot[:, 1, :], start=False, stop=True)
                eng.matmul(B[7][:, 8:12], ones, hot[:, 0, :], start=True, stop=False)
                eng.matmul(B[7][:, 8:12], ones, hot[:, 1, :], start=False, stop=True).then_inc(router_ready, 1)

            def experts(l):
                route(l)
                base = st[f"moe{l}"]
                first = tiles[base]["order"]
                with eng.Fori(0, PASSES) as p:
                    def wait_tile(i):
                        t = tiles[base + i]
                        eng.wait_ge(w_loaded[t["slot"]], t["loaded"] + p * (16 * PASS_TILES // RING))
                        return slot(base + i)
                    experts_pass(moe, p + PASSES * l, wait_tile, None)
                over = eng.value_load(FLAG[0:1, 0:1], min_val=0, max_val=1)
                with eng.If(over == 1):
                    def wait_over(i):
                        eng.wait_ge(ovf_loaded[l][i % RING], 16 * (i // RING + 1))
                        return slot(i)
                    experts_pass(ovf[l], 0, wait_over, None)
                used.n += PASSES * PASS_TILES

            def mixer_out(name, done):
                done()
                turn(name, lambda i, tb: NB[:, tb, i * 128:(i + 1) * 128])
                turns_taken(name)

            eng.wait_ge(consts_loaded, CONSTS)
            for l in range(2):
                if l == 0:
                    turn_normed("mem0")
                else:
                    turn("mem1", lambda i, tb: NB[:, tb, i * 128:(i + 1) * 128])
                    turns_taken("mem1")
                t, qs = st[f"kv{l}"]
                loaded(t)
                wk = slot(t)[:, 0:2048].rearrange("p (k n) -> p k n", k=KD)
                wv = slot(t)[:, 2048:4096].rearrange("p (k n) -> p k n", k=KD)
                for i in range(2):
                    chunk(qs[i], [(wk[:, k, i * 128:(i + 1) * 128], HT[:, k, :]) for k in range(KD)])
                for tb in range(TB):
                    chunk(qs[2 + tb], [(HT[:, k, tb * 128:(tb + 1) * 128], wv[:, k, :]) for k in range(KD)])

            for j in range(12):
                modulation()
            turn_normed("a0h1")
            for j, (t, qs) in enumerate(st["even_in"]):
                v = slot(t).rearrange("p (k n) -> p k n", k=KD)
                loaded(t)
                for tb, q in enumerate(qs):
                    chunk(q, [(HT[:, k, tb * 128:(tb + 1) * 128], v[:, k, :]) for k in range(KD)])
                if j < 6:
                    modulation()
                    modulation()
            P0 = pview(EVEN_IN)
            eng.wait_ge(a0_rotated, 1)
            turn("a0ret", lambda i, tb: P0[:, tb, i * 128:(i + 1) * 128])
            turn("a0att", lambda i, tb: P0[:, tb, 2048 + i * 128:2176 + i * 128])
            turns_taken("a0att")
            for h in range(RET_HEADS):
                if h >= 2:
                    eng.wait_ge(ret_decayed, h - 1)
                b, kT, qT = B[h % 2], QK[:, 4 + h, :], QK[:, h, :]
                eng.matmul(b[:, 0:256], kT[:, 0:128], qT, start=True, stop=True)
                eng.matmul(b[:, 256:384], kT[:, 128:256], qT[:, 128:256], start=True, stop=True)\
                    .then_inc(ret_scores, 1)
            for h in range(RET_HEADS):
                eng.wait_ge(ret_decayed, h + 1)
                if h >= 2:
                    eng.wait_ge(ret_out, h - 1)
                b, s_, v = B[2 + h % 2], SCR[:, h, :], (lambda jb: P0[:, jb, 1024 + 128 * h:1152 + 128 * h])
                eng.matmul(b[:, 0:128], s_[:, 0:128], v(0), start=True, stop=True)
                eng.matmul(b[:, 128:256], s_[:, 128:256], v(0), start=True, stop=False)
                eng.matmul(b[:, 128:256], s_[:, 256:384], v(1), start=False, stop=True).then_inc(ret_values, 1)
            eng.wait_ge(ret_out, 4)
            attention([u for u in units_of("a0", P0)])
            mixer_out("a0mix", lambda: eng.wait_ge(a0_mixed, 1))
            project("even_out")
            turn_normed("a0h2")
            experts(0)

            turn_normed("a1h1")
            project("odd_in")
            P1 = pview(ODD_IN)
            eng.wait_ge(copied["act"], chunks[st["odd_in"][-1][1][-1]]["done"])
            turn("a1qk", lambda i, tb: P1[:, tb, i * 128:(i + 1) * 128])
            turns_taken("a1qk")

            def stick_scores(h):
                if h >= 2:
                    eng.wait_ge(stick_z, h - 1)
                lo = HD * (h % 2)
                kT, qT, b = QK[lo:lo + HD, 8 + h // 2, :], QK[lo:lo + HD, h // 2, :], B[h % 2]
                eng.matmul(b[:, 0:256], kT[:, 0:128], qT, start=True, stop=True)
                eng.matmul(b[:, 256:384], kT[:, 128:256], qT[:, 128:256], start=True, stop=True)\
                    .then_inc(stick_scored, 1)

            def stick_sums(h):
                eng.wait_ge(stick_logs, h + 1)
                if h >= 2:
                    eng.wait_ge(stick_arg, h - 1)
                b, L = B[2 + h % 2], SCR[:, h % 2, :]
                eng.matmul(b[:, 0:256], after, L[:, 0:256], start=True, stop=False)
                eng.matmul(b[:, 128:256], ones, L[:, 256:384], start=False, stop=True)
                eng.matmul(b[:, 256:384], after, L[:, 256:384], start=True, stop=True).then_inc(stick_summed, 1)

            def stick_values(h):
                eng.wait_ge(stick_probs, h + 1)
                if h >= 2:
                    eng.wait_ge(stick_out, h - 1)
                lo, A = HD * (h % 2), SCR[:, 2 + h % 2, :]
                b = B[4 + h % 2]
                v = lambda jb: P1[:, jb, 2048 + HD * h:2048 + HD * (h + 1)]
                eng.matmul(b[lo:lo + HD, 0:256], v(0), A[:, 0:256], start=True, stop=False)
                eng.matmul(b[lo:lo + HD, 128:256], v(1), A[:, 256:384], start=False, stop=True)\
                    .then_inc(stick_valued, 1)

            for t in range(STICKS + 2):
                if t < STICKS:
                    stick_scores(t)
                if 1 <= t <= STICKS:
                    stick_sums(t - 1)
                if t >= 2:
                    stick_values(t - 2)
            eng.wait_ge(stick_out, STICKS)
            project("odd_out")
            turn_normed("a1h2")
            experts(1)

            turn_normed("b0h0")
            project("ev_in", EV_IN)
            P2 = pview(EV_IN)
            eng.wait_ge(b0_roped, 1)
            KD4 = AUX[:, 4096:5120].rearrange("p (t x n) -> p t x n", t=TB, x=4)

            def b0_source(i, tb):
                if i < 8:
                    return P2[:, tb, i * 128:(i + 1) * 128]
                if i < 12:
                    return P2[:, tb, 1544 + (i - 8) * 128:1544 + (i - 7) * 128]
                return KD4[:, tb, i - 12, :]
            turn("b0qk", b0_source)
            LF = ST[:, 0:256].rearrange("p (t n) -> p t n", t=TB)
            eng.matmul(B[6][:, 0:128], LF[:, 0, :], upto, start=True, stop=True)
            eng.matmul(B[6][:, 128:256], LF[:, 0, :], ones, start=True, stop=False)
            eng.matmul(B[6][:, 128:256], LF[:, 1, :], upto, start=False, stop=True).then_inc(gates_summed, 1)
            turns_taken("b0qk")
            for i, at in enumerate((2056, 2184)):
                for r in range(2):
                    for g in range(2):
                        for tb in range(TB):
                            mm = eng.matmul(B[i][r * HD:(r + 1) * HD, g * 128 + tb * 64:g * 128 + (tb + 1) * 64],
                                            P2[:, tb, at + g * HD:at + (g + 1) * HD],
                                            ident.rearrange("p (m r) -> p r m", r=2)[:, r, :],
                                            start=True, stop=True)
            mm.then_inc(cmp_pe, 1)
            t = st["cmp"]
            loaded(t)
            w1 = slot(t).rearrange("p (i k n) -> p i k n", i=2, k=16)
            XS = [AUX[:, 4096 + 496 * i:4592 + 496 * i].rearrange("p (k n) -> p k n", k=16) for i in range(2)]
            eng.wait_ge(cmp_dve, 1)
            for i in range(2):
                for k in range(16):
                    mm = eng.matmul(B[2 + i][:, 0:31], w1[:, i, k, :], XS[i][:, k, :], start=(k == 0), stop=(k == 15))
            mm.then_inc(*used.up())
            HC = ST[:, 0:60]
            eng.wait_ge(cmp_dve, 3)
            eng.matmul(B[0][:, 0:30], W2K, HC[:, 0:30], start=True, stop=True)
            for g in range(2):
                mm = eng.matmul(B[1][0:CMP_N, g * HD:(g + 1) * HD], HC[:, 30 + 15 * g:45 + 15 * g], W2V,
                                start=True, stop=True)
            mm.then_inc(cmp_pe, 1)
            eng.wait_ge(cmp_act, 2)
            eng.matmul(B[2][:, 0:128], REP[0:CMP_N, :], VC[0:CMP_N, :], start=True, stop=True).then_inc(cmp_pe, 1)
            for par in range(2):
                for tb in range(TB):
                    for i in range(4):
                        h = 2 * i + par
                        mm = eng.matmul(B[4 + par][:, (tb * 4 + i) * 16:(tb * 4 + i) * 16 + CMP_N],
                                        QK[HD * par:HD * (par + 1), 8 + i, tb * 128:(tb + 1) * 128],
                                        KC[HD * par:HD * (par + 1), (h // 4) * 15:(h // 4) * 15 + CMP_N],
                                        start=True, stop=True)
            mm.then_inc(cmp_pe, 1)
            eng.wait_ge(cmp_dve, 5)
            for tb in range(TB):
                mm = eng.transpose(B[3][:, tb * 128:(tb + 1) * 128], CP[:, tb, :], ident)
            mm.then_inc(cmp_pe, 1)
            eng.wait_ge(cmp_act, 4)
            for tb in range(TB):
                mm = eng.matmul(B[6 + tb][:, :], PCT[:, tb * 128:(tb + 1) * 128], VB, start=True, stop=True)
            mm.then_inc(cmp_pe, 1)
            eng.wait_ge(cmp_act, 5)
            eng.wait_ge(aux_loaded, 16 * 4)
            attention(units_of("b0", P2))
            mixer_out("b0mix", lambda: eng.wait_ge(head_done, UNITS["b0"][1]))
            project("ev_out")

            def cross(l):
                turn_normed(f"b{l}h2")
                t, qs = st[f"caq{l}"]
                loaded(t)
                wq = slot(t)[:, 0:2048].rearrange("p (k n) -> p k n", k=KD)
                for i in range(2):
                    chunk(qs[i], [(wq[:, k, i * 128:(i + 1) * 128], HT[:, k, :]) for k in range(KD)])
                eng.wait_ge(copied["act"], chunks[qs[1]]["done"])
                attention(units_of(f"ca{l}", None))
                mixer_out(f"b{l}ca", lambda: eng.wait_ge(head_done, UNITS[f"ca{l}"][1]))
                wo = slot(t)[:, 2048:4096].rearrange("p (k n) -> p k n", k=2)
                for i, q in enumerate(st[f"cao{l}"][1]):
                    tb, h = i // 2, i % 2
                    chunk(q, [(HT[:, k, tb * 128:(tb + 1) * 128], wo[:, k, h * 512:(h + 1) * 512]) for k in range(2)])

            def feed_forward(l):
                turn_normed(f"b{l}h4")
                last_q = st[f"cao{l}"][1][-1]
                eng.wait_ge(copied["act"], chunks[last_q]["done"])
                base = st[f"ffn{l}"]
                n0 = 2 * FFN_STEPS * l

                def gate_up(wait, n, s, first, hbuf):
                    wait()
                    v = slot(n).rearrange("p (i k n) -> p i k n", i=2, k=KD)
                    for f in range(2):
                        for i in range(2):
                            if not first:
                                eng.wait_ge((ffn_silu, ffn_he)[i], s * 2 + (n0 - 2 + f + 1))
                            for k in range(KD):
                                mm = eng.matmul(B[2 * i + f][:, 0:S], v[:, i, k, f * 128:(f + 1) * 128], HT[:, k, :],
                                                start=(k == 0), stop=(k == KD - 1))
                            if i == 0:
                                mm.then_inc(ffn_gate, 1)
                            elif f == 0:
                                mm.then_inc(ffn_up, 1)
                            else:
                                mm.then_inc(weights_used, 1)

                def down(wait, n, s, first, last, par):
                    wait()
                    v = slot(n)[:, 0:2048].rearrange("p (k n) -> p k n", k=2)
                    eng.wait_ge(ffn_he, s * 2 + (n0 + 2))
                    for k in range(2):
                        for tb in range(TB):
                            for h in range(2):
                                mm = eng.matmul(B[4 + 2 * tb + h][:, :], FHE[2 * par + k][:, tb * 128:(tb + 1) * 128],
                                                v[:, k, h * 512:(h + 1) * 512], start=(first and k == 0),
                                                stop=(last and k == 1), skip_group_check=True)
                    mm.then_inc(weights_used, 1)

                gate_up(lambda: loaded(base), base, 0, l == 0, 0)
                n = base + 1
                pairs = (FFN_STEPS - 1) // 2
                delta = [tiles[n + 4 + j]["loaded"] - tiles[n + j]["loaded"] for j in range(4)]
                for i in range(1):
                    gate_up(lambda: loaded(n), n, 1, False, 1)
                    down(lambda: loaded(n + 1), n + 1, 0, True, False, 0)
                    gate_up(lambda: loaded(n + 2), n + 2, 2, False, 0)
                    down(lambda: loaded(n + 3), n + 3, 1, False, False, 1)
                with eng.Fori(1, pairs) as i:
                    def wait(j):
                        return lambda: eng.wait_ge(w_loaded[tiles[n + j]["slot"]], tiles[n + j]["loaded"] + i * delta[j])
                    gate_up(wait(0), n, i * 2 + 1, False, 1)
                    down(wait(1), n + 1, i * 2, False, False, 0)
                    gate_up(wait(2), n + 2, i * 2 + 2, False, 0)
                    down(wait(3), n + 3, i * 2 + 1, False, False, 1)
                end = base + 2 * FFN_STEPS - 1
                down(lambda: loaded(end), end, FFN_STEPS - 1, False, True, 0)
                used.n += 2 * FFN_STEPS

            cross(0)
            feed_forward(0)

            turn_normed("b1h0")
            project("od_in")
            P3 = pview(OD_IN)
            eng.wait_ge(b1_roped, 1)
            turn("b1qk", lambda i, tb: P3[:, tb, i * 128:(i + 1) * 128])
            turns_taken("b1qk")
            attention(units_of("b1", P3))
            mixer_out("b1mix", lambda: eng.wait_ge(b1_mixed, 1))
            project("od_out")
            cross(1)
            feed_forward(1)

        @block.scalar
        def _(eng):
            done = Count(act_done)
            told = Count(told_act)
            roots, asked, sq = [0], [0], [0]
            unit, vunit = [0], [0]

            eng.dma_start(PR[:, 0:2048].rearrange("p (t n) -> p t n", t=TB),
                          a["mem_2"].rearrange("b (t p) d -> p (b t) d", p=128)).then_inc(mem_loaded, 16)
            eng.dma_start(X[:, :, :], a["x"].rearrange("b (t p) d -> p (b t) d", p=128)).then_inc(x_loaded, 16)
            for dst, src in ((CF[:, :], a["c_fm"]), (CS[:, :], a["consts"]), (GM[:, :, :], a["gains_fm"]),
                             (ABF[:, :, :], a["ada_b_fm"]), (AG[:, :], a["qk_gains"]), (RW[:, :, :], cols(a["router_w"], 0, 16)),
                             (RB[:, :], a["router_b"].partition_broadcast(128)), (POS[:, :, :], a["cmp_pos"]),
                             (W2[:, :], a["cmp_w2"]), (GB[:, :, :], a["gate_bias"].partition_broadcast(128)),
                             (decay, a["decay"]), (bias, a["rel_bias"]), (PI[:, :], a["positions_fm"]),
                             (FB[:, :], a["fox_bias"].partition_broadcast(128))):
                eng.dma_start(dst, src).then_inc(consts_loaded, 16)

            def take_turned(name, dst, affine=None):
                first, items = turns[name]
                for i in range(items):
                    x = first + i
                    if x % 2 == 0:
                        eng.wait_ge(turned, x + 1)
                        if affine is None:
                            ins = eng.activation(dst(i), B[x % 4][:, 0:S], ACT.Copy)
                        else:
                            g, s = affine(i)
                            if s is None:
                                ins = eng.activation(dst(i), B[x % 4][:, 0:S], ACT.Copy, scale=g)
                            else:
                                ins = eng.activation(dst(i), B[x % 4][:, 0:S], ACT.Identity, scale=g, bias=s)
                        ins.then_inc(turn_taken[0], 1)

            def take_chunks(qs, dst):
                for i, q in enumerate(qs):
                    c = chunks[q]
                    if c["evac"] == "act":
                        eng.wait_ge(S_[c["ready"][0]], c["ready"][1])
                        o = dst(i)
                        eng.activation(o, B[4 + q % 2][:, 0:o.shape[-1]], ACT.Copy).then_inc(copied["act"], 1)

            def take_project(name, dst):
                for j, (t, qs) in enumerate(st[name]):
                    take_chunks(qs, lambda i: dst(j, i))

            def squares_of(src):
                for tb in range(TB):
                    eng.activation(NB[:, tb, :], src(tb), ACT.Square, accum_out=SS[:, tb:tb + 1]).then_inc(squares, 1)

            def root(width):
                roots[0] += 1
                eng.wait_ge(var_ready, roots[0])
                eng.activation(ROOT[:, 0:width], VAR[:, 0:width], ACT.Sqrt).then_inc(root_ready, 1)

            def norm_x(n):
                if n:
                    eng.wait_ge(x_ready, n)
                else:
                    eng.wait_ge(x_loaded, 16)
                squares_of(lambda tb: X[:, tb, :])
                root(TB)

            def await_ask():
                asked[0] += 1
                eng.wait_ge(ask_act, asked[0])

            def attention(units):
                n, u0, v0 = len(units), unit[0], vunit[0]
                per = len(units[0]["scores"])
                unit[0] += n * per
                vunit[0] += n
                for t in range(n + 1):
                    if t < n:
                        d = units[t]
                        for j in range(per):
                            u = u0 + t * per + j
                            eng.wait_ge(shifted, u + 1)
                            if per == 1 and t >= 2:
                                eng.wait_ge(probs_turned, v0 + t - 1)
                            if per == 2 and t >= 1:
                                eng.wait_ge(probs_joined, t)
                            eng.activation(SCR[:, 2 + u % 2, 0:d["nk"]], SCR[:, u % 2, 0:d["nk"]], ACT.Exp,
                                           scale=-1.0, bias=ST[:, 312 + u % 4:313 + u % 4],
                                           accum_out=ST[:, 316 + u % 4:317 + u % 4]).then_inc(probs_ready, 1)
                    if t >= 1:
                        v, d = v0 + t - 1, units[t - 1]
                        eng.wait_ge(probs_turned, v + 1)
                        if v >= 2:
                            eng.wait_ge(values_ready, v - 1)
                        eng.activation(SCR[:, 4 + v % 2, 0:d["nk"]], B[2 + v % 2][:, 0:d["nk"]], ACT.Copy)\
                           .then_inc(probs_copied, 1)

            def experts_pass(m, P, tile_order):
                eng.wait_ge(m["gathered"], P * 2 + 1)
                for k in range(4):
                    ins = eng.activation(XG[:, k, :], B[0][:, k * 128:(k + 1) * 128], ACT.Identity,
                                         scale=SCL[:, nidx[0], k:k + 1], bias=SHF[0][:, k:k + 1])
                    if k == 3:
                        ins.then_inc(m["feat_act"], 1)
                eng.wait_ge(m["back_ready"], P + 1)
                eng.activation(BACK, B[3][:, 0:S], ACT.Copy).then_inc(m["back_copied"], 1)

                def silu(e):
                    eng.wait_ge(m["used"], tile_order("g", e))
                    if e >= 2:
                        eng.wait_ge(m["hidden"], P * 4 + (e - 1))
                    eng.activation(SG[e % 2], B[4 + 2 * (e % 2)][:, :], ACT.Silu).then_inc(m["silu"], 1)

                def copy_turned(e):
                    eng.wait_ge(m["turned"], P * 4 + (e + 1))
                    if e >= 2:
                        eng.wait_ge(m["used"], tile_order("d", e - 2))
                    eng.activation(HET[e % 2], B[2 + e % 2][:, :], ACT.Copy).then_inc(m["turned_copied"], 1)

                silu(0)
                silu(1)
                copy_turned(0)
                silu(2)
                copy_turned(1)
                silu(3)
                copy_turned(2)
                copy_turned(3)
                eng.wait_ge(m["used"], tile_order("d", 3))
                eng.activation(YE[:, 0:512], B[0][:, :], ACT.Copy).then_inc(m["y_act"], 1)

            nidx, SHF = [0], [None]

            def experts(l):
                eng.wait_ge(router_ready, 2 * l + 1)
                eng.activation(ST[:, 0:32], B[6][:, 0:32], ACT.Sigmoid).then_inc(*told.up())
                nidx[0] = 2 * l + 1
                SHF[0] = MOD[:, l, 24:32]
                first = tiles[st[f"moe{l}"]]["order"]
                with eng.Fori(0, PASSES) as p:
                    experts_pass(moe, p + PASSES * l,
                                 lambda kind, e: p * PASS_TILES + (first + PLACE[kind, e] + 1))
                over = eng.value_load(FLAG[0:1, 0:1], min_val=0, max_val=1)
                with eng.If(over == 1):
                    experts_pass(ovf[l], 0, lambda kind, e: PLACE[kind, e] + 1)

            def feature(i):
                return HT[:, i, :]

            eng.wait_ge(mem_loaded, 16)
            squares_of(lambda tb: PR[:, tb * D:(tb + 1) * D])
            root(TB)
            eng.wait_ge(consts_loaded, CONSTS)
            eng.activation(CF[:, :], CF[:, :], ACT.Silu).then_inc(*told.up())
            for l in range(2):
                take_turned(f"mem{l}", feature, lambda i, l=l: (GM[:, 10 + l, i:i + 1], None))
                take_chunks(st[f"kv{l}"][1], lambda i, l=l: MK[:, l, i, :] if i < 2 else MV[:, l, i - 2, :])
            norm_x(0)
            eng.wait_ge(scales_ready, 1)
            take_turned("a0h1", feature, lambda i: (SCL[:, 0, i:i + 1], MOD[:, 0, i:i + 1]))
            P0 = pview(EVEN_IN)
            take_project("even_in", lambda j, tb: P0[:, tb, j * 512:(j + 1) * 512])
            root(32)
            take_turned("a0ret", lambda i: QK[:, i, :])
            take_turned("a0att", lambda i: QK[:, 8 + i, :], lambda i: (AG[:, i // 4:i // 4 + 1], None))
            for h in range(RET_HEADS):
                eng.wait_ge(ret_values, h + 1)
                eng.activation(NB[:, :, h * 128:(h + 1) * 128], B[2 + h % 2][:, 0:256].rearrange("p (t n) -> p t n", t=TB),
                               ACT.Copy).then_inc(ret_out, 1)
            eng.activation(P0[:, :, 1536:2048], P0[:, :, 1536:2048], ACT.Silu).then_inc(*told.up())
            root(8)
            attention(units_of("a0", P0))
            take_turned("a0mix", feature)
            norm_x(1)
            eng.wait_ge(scales_ready, 2)
            take_turned("a0h2", feature, lambda i: (SCL[:, 1, i:i + 1], MOD[:, 0, 24 + i:25 + i]))
            experts(0)

            norm_x(2)
            take_turned("a1h1", feature, lambda i: (SCL[:, 2, i:i + 1], MOD[:, 1, i:i + 1]))
            P1 = pview(ODD_IN)
            take_project("odd_in", lambda j, tb: P1[:, tb, j * 512:(j + 1) * 512])
            take_turned("a1qk", lambda i: QK[:, i, :])
            ZS = [AUX[:, 384 * i:384 * (i + 1)] for i in range(2)]
            LG = [AUX[:, 768 + 384 * i:1152 + 384 * i] for i in range(2)]
            WT = [AUX[:, 1536 + 384 * i:1920 + 384 * i] for i in range(2)]
            AE = [AUX[:, 2304 + 384 * i:2688 + 384 * i] for i in range(2)]
            for t in range(STICKS + 2):
                if t < STICKS:
                    eng.wait_ge(stick_scored, t + 1)
                    if t >= 2:
                        eng.wait_ge(stick_arg, t - 1)
                    z, g = ZS[t % 2], LG[t % 2]
                    eng.activation(z, B[t % 2][:, 0:384], ACT.Copy, scale=HD ** -0.5).then_inc(stick_z, 1)
                    eng.wait_ge(stick_z, t + 1)
                    eng.activation(g, z, ACT.Abs).then_inc(*done.up())
                    eng.wait_ge(*done.now())
                    eng.activation(g, g, ACT.Exp, scale=-1.0).then_inc(*done.up())
                    eng.wait_ge(*done.now())
                    eng.activation(g, g, ACT.Ln, bias=1.0).then_inc(stick_log, 1)
                if 1 <= t <= STICKS:
                    h = t - 1
                    eng.wait_ge(stick_arg, h + 1)
                    if h >= 2:
                        eng.wait_ge(stick_probs, h - 1)
                    eng.activation(AE[h % 2], WT[h % 2], ACT.Exp).then_inc(stick_exp, 1)
                if t >= 2:
                    h = t - 2
                    lo = HD * (h % 2)
                    eng.wait_ge(stick_valued, h + 1)
                    eng.activation(HT[lo:lo + HD, h // 2, :], B[4 + h % 2][lo:lo + HD, 0:S], ACT.Copy)\
                       .then_inc(stick_out, 1)
            norm_x(3)
            take_turned("a1h2", feature, lambda i: (SCL[:, 3, i:i + 1], MOD[:, 1, 24 + i:25 + i]))
            experts(1)

            norm_x(4)
            take_turned("b0h0", feature, lambda i: (GM[:, 4, i:i + 1], None))
            P2 = pview(EV_IN)
            take_project("ev_in", lambda j, tb: P2[:, tb, j * 512:min(EV_IN, (j + 1) * 512)])
            eng.wait_ge(*((copied["act"], chunks[st["ev_in"][-1][1][-1]]["done"])))
            eng.activation(GT, P2[:, :, 2824:2848], ACT.Sigmoid).then_inc(*told.up())
            await_ask()
            eng.activation(SCR[:, 0, 0:32], SCR[:, 0, 0:32], ACT.Sin).then_inc(*told.up())
            await_ask()
            eng.activation(SCR[:, 1, 0:16], SCR[:, 1, 0:16], ACT.Exp, scale=-1.0).then_inc(*done.up())
            eng.wait_ge(*done.now())
            eng.activation(SCR[:, 1, 0:16], SCR[:, 1, 0:16], ACT.Ln, bias=1.0).then_inc(*told.up())
            take_turned("b0qk", lambda i: QK[:, i, :])
            eng.wait_ge(gates_summed, 1)
            eng.activation(CT, B[6][:, 0:S], ACT.Copy).then_inc(gates_copied, 1)
            eng.wait_ge(cmp_dve, 2)
            eng.activation(ST[:, 60:120], ST[:, 60:120], ACT.Tanh, scale=0.7978845608028654).then_inc(cmp_act, 1)
            eng.wait_ge(cmp_pe, 2)
            eng.activation(KC, B[0][:, 0:30], ACT.Copy).then_inc(*done.up())
            eng.activation(VC[0:CMP_N, :], B[1][0:CMP_N, 0:128], ACT.Copy).then_inc(cmp_act, 1)
            eng.wait_ge(cmp_dve, 4)
            eng.activation(CP, CP, ACT.Exp).then_inc(cmp_act, 1)
            eng.wait_ge(cmp_pe, 5)
            eng.activation(PCT, B[3][:, 0:S], ACT.Copy).then_inc(cmp_act, 1)
            eng.wait_ge(cmp_pe, 6)
            eng.activation(NB[:, 0, 512:1024], B[6][:, :], ACT.Copy).then_inc(*done.up())
            eng.activation(NB[:, 1, 512:1024], B[7][:, :], ACT.Copy).then_inc(cmp_act, 1)
            attention(units_of("b0", P2))
            take_turned("b0mix", feature)
            take_project("ev_out", lambda j, tb: Y[:, tb, j * 512:(j + 1) * 512])

            def norm_y(ready):
                ready()
                squares_of(lambda tb: Y[:, tb, :])
                root(TB)

            def chunks_taken(q):
                return lambda: eng.wait_ge(copied["act"], chunks[q]["done"])

            def cross(l, n):
                norm_x(n)
                take_turned(f"b{l}h2", feature, lambda i: (GM[:, 5 + 3 * l, i:i + 1], None))
                take_chunks(st[f"caq{l}"][1], lambda i: QK[:, i, :])
                attention(units_of(f"ca{l}", None))
                take_turned(f"b{l}ca", feature)
                take_chunks(st[f"cao{l}"][1], lambda i: Y[:, i // 2, (i % 2) * 512:(i % 2 + 1) * 512])
                norm_y(chunks_taken(st[f"cao{l}"][1][-1]))

            def feed_forward(l, n):
                norm_x(n)
                take_turned(f"b{l}h4", feature, lambda i: (GM[:, 6 + 3 * l, i:i + 1], None))
                n0 = 2 * FFN_STEPS * l

                def silu(s, first):
                    for f in range(2):
                        eng.wait_ge(ffn_gate, s * 2 + (n0 + f + 1))
                        if not first:
                            eng.wait_ge(ffn_he, s * 2 + (n0 - 2 + f + 1))
                        eng.activation(FSG[f], B[f][:, 0:S], ACT.Silu).then_inc(ffn_silu, 1)
                silu(0, l == 0)
                with eng.Fori(1, FFN_STEPS) as s:
                    silu(s, False)
                end = tiles[st[f"ffn{l}"] + 2 * FFN_STEPS - 1]["order"] + 1
                eng.wait_ge(weights_used, end)
                for i in range(4):
                    eng.activation(Y[:, i // 2, (i % 2) * 512:(i % 2 + 1) * 512], B[4 + i][:, :], ACT.Copy)\
                       .then_inc(*done.up())
                norm_y(lambda: eng.wait_ge(*done.now()))

            norm_y(chunks_taken(st["ev_out"][-1][1][-1]))
            cross(0, 5)
            feed_forward(0, 6)

            norm_x(7)
            take_turned("b1h0", feature, lambda i: (GM[:, 7, i:i + 1], None))
            P3 = pview(OD_IN)
            take_project("od_in", lambda j, tb: P3[:, tb, j * 512:(j + 1) * 512])
            await_ask()
            eng.activation(VAR[:, 30:32], VAR[:, 30:32], ACT.Exp).then_inc(*told.up())
            take_turned("b1qk", lambda i: QK[:, i, :])
            attention(units_of("b1", P3))
            root(16)
            take_turned("b1mix", feature, lambda i: (AG[:, 2:3], None))
            take_project("od_out", lambda j, tb: Y[:, tb, j * 512:(j + 1) * 512])
            norm_y(chunks_taken(st["od_out"][-1][1][-1]))
            cross(1, 8)
            feed_forward(1, 9)

        @block.vector
        def _(eng):
            vec = Count(vec_done)
            V = eng.tensor_tensor
            told, roots, sqn = [0], [0], [0]
            unit, vunit, joined = [0], [0], [0]

            def settle():
                eng.wait_ge(*vec.now())

            def await_act():
                told[0] += 1
                eng.wait_ge(told_act, told[0])

            def wide(ap, *shape):
                return ap.to_broadcast(list(shape))

            def take_turned(name, dst, affine=None):
                first, items = turns[name]
                for i in range(items):
                    x = first + i
                    if x % 2 == 1:
                        eng.wait_ge(turned, x + 1)
                        if affine is None:
                            ins = eng.tensor_copy(dst(i), B[x % 4][:, 0:S])
                        else:
                            g, s = affine(i)
                            if s is None:
                                ins = eng.tensor_scalar(dst(i), B[x % 4][:, 0:S], g, None, ALU.mult)
                            else:
                                ins = eng.tensor_scalar(dst(i), B[x % 4][:, 0:S], g, s, ALU.mult, ALU.add)
                        ins.then_inc(turn_taken[1], 1)

            def root(width, count):
                roots[0] += 1
                eng.tensor_scalar(VAR[:, 0:width], VAR[:, 0:width], 1.0 / count, EPS, ALU.mult, ALU.add)\
                   .then_inc(var_ready, 1)
                eng.wait_ge(root_ready, roots[0])
                eng.reciprocal(RSD[:, 0:width], ROOT[:, 0:width]).then_inc(*vec.up())
                settle()

            def squares_root():
                sqn[0] += TB
                eng.wait_ge(squares, sqn[0])
                eng.tensor_copy(VAR[:, 0:TB], SS[:, 0:TB]).then_inc(*vec.up())
                settle()
                root(TB, D)

            def normalise(src):
                squares_root()
                for tb in range(TB):
                    ins = eng.tensor_scalar(NB[:, tb, :], src(tb), RSD[:, tb:tb + 1], None, ALU.mult)
                ins.then_inc(normed, 1)

            def norm_x():
                normalise(lambda tb: X[:, tb, :])

            def add_projected(name, gate, done):
                for j, (t, qs) in enumerate(st[name]):
                    for tb, q in enumerate(qs):
                        c = chunks[q]
                        eng.wait_ge(S_[c["ready"][0]], c["ready"][1])
                        tmp = PR[:, (q % 4) * 512:(q % 4 + 1) * 512]
                        V(tmp, B[4 + q % 2][:, :], GB[:, gate, j * 512:(j + 1) * 512], ALU.mult).then_inc(copied["dve"], 1)
                        eng.wait_ge(copied["dve"], c["done"])
                        xs = X[:, tb, j * 512:(j + 1) * 512]
                        V(xs, xs, tmp, ALU.add).then_inc(*vec.up())
                settle()
                finish_x()

            def finish_x():
                eng.memset(FINI[:, :], 0.0).then_inc(x_ready, 1)

            def add_normed_y(gain):
                squares_root()
                for tb in range(TB):
                    eng.scalar_tensor_tensor(out=NB[:, tb, :], in0=Y[:, tb, :], scalar=RSD[:, tb:tb + 1], in1=GB[:, gain, :],
                                             op0=ALU.mult, op1=ALU.mult).then_inc(*vec.up())
                settle()
                V(X[:, :, :], X[:, :, :], NB[:, :, :], ALU.add).then_inc(x_ready, 1)

            def rotate(v, cos, sin, half, tmp):
                x1, x2 = v[..., 0:half], v[..., half:2 * half]
                for dst, x, f in ((tmp[0], x1, cos), (tmp[1], x2, sin), (tmp[2], x1, sin), (tmp[3], x2, cos)):
                    V(dst, x, f, ALU.mult).then_inc(*vec.up())
                settle()
                V(x1, tmp[0], tmp[1], ALU.subtract).then_inc(*vec.up())
                V(x2, tmp[2], tmp[3], ALU.add).then_inc(*vec.up())
                settle()

            def attention(units):
                n, u0, v0 = len(units), unit[0], vunit[0]
                per = len(units[0]["scores"])
                unit[0] += n * per
                vunit[0] += n
                for t in range(n + 2):
                    if t < n:
                        d = units[t]
                        for j in range(per):
                            u = u0 + t * per + j
                            eng.wait_ge(scores_ready, u + 1)
                            if u >= 2:
                                eng.wait_ge(probs_ready, u - 1)
                            eng.tensor_tensor_reduce(SCR[:, u % 2, 0:d["nk"]], B[u % 2][:, 0:d["nk"]], d["mask"],
                                                     -d["scale"], 3.0e38, ALU.add, ALU.min,
                                                     ST[:, 312 + u % 4:313 + u % 4]).then_inc(shifted, 1)
                    if 1 <= t <= n:
                        d, v = units[t - 1], v0 + t - 1
                        last = u0 + t * per
                        eng.wait_ge(probs_ready, last)
                        r = RC[:, 2 * (v % 4):2 * (v % 4) + per]
                        at = 316 + (last - per) % 4
                        eng.reciprocal(r, ST[:, at:at + per]).then_inc(*vec.up())
                        if d["gate"] is not None:
                            settle()
                            V(r, r, d["gate"], ALU.mult).then_inc(*vec.up())
                        if per == 2:
                            settle()
                            V(r[:, 1:2], r[:, 1:2], LAM, ALU.mult).then_inc(*vec.up())
                            if v - v0 >= 2:
                                eng.wait_ge(probs_turned, v - 1)
                            p, nk = SCR[:, 6 + (t - 1) % 2, 0:d["nk"]], d["nk"]
                            eng.tensor_scalar(p, SCR[:, 2 + (last - 2) % 2, 0:nk], r[:, 0:1], None, ALU.mult)\
                               .then_inc(*vec.up())
                            settle()
                            eng.scalar_tensor_tensor(out=p, in0=SCR[:, 2 + (last - 1) % 2, 0:nk], scalar=r[:, 1:2],
                                                     in1=p, op0=ALU.mult, op1=ALU.add).then_inc(probs_joined, 1)
                            joined[0] += 1
                    if t >= 2:
                        d, v = units[t - 2], v0 + t - 2
                        eng.wait_ge(values_ready, v + 1)
                        settle()
                        b, r = B[4 + v % 2][:, 0:d["out"].shape[-1]], RC[:, 2 * (v % 4):2 * (v % 4) + 1]
                        if per == 2:
                            ins = eng.tensor_copy(d["out"], b)
                        elif d["add"]:
                            eng.wait_ge(head_done, v)
                            ins = eng.scalar_tensor_tensor(out=d["out"], in0=b, scalar=r, in1=d["out"], op0=ALU.mult,
                                                           op1=ALU.add)
                        else:
                            ins = eng.tensor_scalar(d["out"], b, r, None, ALU.mult)
                        ins.then_inc(head_done, 1)

            ada = [0]

            def ada_sum():
                j = ada[0]
                ada[0] += 1
                n = (st["ada0"] + st["ada1"])[j]
                w = slot(n).rearrange("p (k n) -> p k n", k=KD)
                acc = ACC[:, j % 2, :]
                eng.wait_ge(w_loaded[tiles[n]["slot"]], tiles[n]["loaded"])
                if j >= 2:
                    eng.wait_ge(mod_ready, j - 1)
                eng.tensor_scalar(acc, w[:, 0, :], CF[:, 0:1], None, ALU.mult).then_inc(*vec.up())
                for k in range(1, KD):
                    settle()
                    ins = eng.scalar_tensor_tensor(out=acc, in0=w[:, k, :], scalar=CF[:, k:k + 1], in1=acc,
                                                   op0=ALU.mult, op1=ALU.add)
                    ins.then_inc(*(vec.up() if k < KD - 1 else (ada_summed, 1)))
                if j % 12:
                    ada_take(j - 1)

            def ada_take(j):
                l, i = j // 12, j % 12
                eng.wait_ge(mod_ready, j + 1)
                if i // 2 in (2, 5):
                    g = GB[:, 2 * l + (i // 2 == 5), (i % 2) * 512:(i % 2 + 1) * 512]
                    V(g, B[6 + j % 2][:, :], g, ALU.add).then_inc(mod_taken, 1)
                else:
                    V(MOD[:, l, 4 * i:4 * i + 4], B[6 + j % 2][:, 0:4], ABF[:, l, 4 * i:4 * i + 4], ALU.add)\
                        .then_inc(mod_taken, 1)

            def scales(l):
                eng.wait_ge(mod_taken, 12 * (l + 1))
                for i in range(2):
                    eng.scalar_tensor_tensor(out=SCL[:, 2 * l + i, :], in0=MOD[:, l, 8 + 24 * i:16 + 24 * i], scalar=1.0,
                                             in1=GM[:, 2 * l + i, :], op0=ALU.add, op1=ALU.mult).then_inc(scales_ready, 1)

            def route(l):
                sc, sel = ST[:, 0:32], ST[:, 32:64]
                v4 = lambda ap: ap.rearrange("p (t g j) -> p t g j", t=TB, g=GROUPS)
                await_act()
                V(sel.rearrange("p (t e) -> p t e", t=TB), sc.rearrange("p (t e) -> p t e", t=TB),
                  wide(RB[:, :].unsqueeze(1), 128, TB, EXPERTS), ALU.add).then_inc(*vec.up())
                settle()
                G = [SCR[:, tb, 0:64].rearrange("p (g j i) -> p g j i", g=4, j=4) for tb in range(TB)]
                E = [SCR[:, 2 + tb, 0:64].rearrange("p (g j i) -> p g j i", g=4, j=4) for tb in range(TB)]
                other = [wide(v4(sel)[:, tb].unsqueeze(2), 128, 4, 4, 4) for tb in range(TB)]
                own = [wide(v4(sel)[:, tb].unsqueeze(3), 128, 4, 4, 4) for tb in range(TB)]
                for tb in range(TB):
                    V(G[tb], other[tb], own[tb], ALU.is_gt).then_inc(*vec.up())
                    V(E[tb], other[tb], own[tb], ALU.is_equal).then_inc(*vec.up())
                settle()
                for tb in range(TB):
                    V(E[tb], E[tb], wide(lower44.unsqueeze(1), 128, 4, 4, 4), ALU.mult).then_inc(*vec.up())
                settle()
                for tb in range(TB):
                    V(G[tb], G[tb], E[tb], ALU.add).then_inc(*vec.up())
                settle()
                top = ST[:, 64:96]
                for tb in range(TB):
                    eng.tensor_reduce(v4(top)[:, tb], G[tb], AX.X, ALU.add).then_inc(*vec.up())
                settle()
                eng.tensor_scalar(top, top, 2.0, None, ALU.is_lt).then_inc(*vec.up())
                settle()
                kept, gs = ST[:, 96:128], ST[:, 128:136].rearrange("p (t g) -> p t g", t=TB)
                V(kept, top, sel, ALU.mult).then_inc(*vec.up())
                settle()
                eng.tensor_reduce(gs, v4(kept), AX.X, ALU.add).then_inc(*vec.up())
                settle()
                best = ST[:, 136:138]
                eng.tensor_reduce(best, gs, AX.X, ALU.max).then_inc(*vec.up())
                settle()
                mark = ST[:, 140:148].rearrange("p (t g) -> p t g", t=TB)
                V(mark, gs, wide(best.unsqueeze(2), 128, TB, GROUPS), ALU.is_ge).then_inc(*vec.up())
                settle()
                i4 = wide(iota4.unsqueeze(1), 128, TB, GROUPS)
                eng.scalar_tensor_tensor(out=mark, in0=mark, scalar=-8.0, in1=i4, op0=ALU.mult, op1=ALU.add)\
                   .then_inc(*vec.up())
                settle()
                gid = ST[:, 148:150]
                eng.tensor_reduce(gid, mark, AX.X, ALU.min).then_inc(*vec.up())
                settle()
                hot = ST[:, 256:264].rearrange("p (t g) -> p t g", t=TB)
                V(hot, mark, wide(gid.unsqueeze(2), 128, TB, GROUPS), ALU.is_equal).then_inc(groups_chosen, 1)
                eng.wait_ge(groups_chosen, l + 1)
                wt = ST[:, 160:192]
                V(wt, top, sc, ALU.mult).then_inc(*vec.up())
                settle()
                for tb in range(TB):
                    V(v4(wt)[:, tb], v4(wt)[:, tb], wide(hot[:, tb].unsqueeze(2), 128, 4, 4), ALU.mult).then_inc(*vec.up())
                settle()
                den, c4 = ST[:, 192:194], ST[:, 196:204].rearrange("p (t j) -> p t j", t=TB)
                eng.tensor_reduce(den, wt.rearrange("p (t e) -> p t e", t=TB), AX.X, ALU.add).then_inc(*vec.up())
                eng.tensor_reduce(c4, wt.rearrange("p (t g j) -> p t j g", t=TB, g=GROUPS), AX.X, ALU.add).then_inc(*vec.up())
                settle()
                eng.reciprocal(den, den).then_inc(*vec.up())
                settle()
                V(CMB[:, :, :], c4, wide(den.unsqueeze(2), 128, TB, PER_GROUP), ALU.mult).then_inc(*vec.up())
                eng.wait_ge(router_ready, 2 * l + 2)
                rk, pos = ST[:, 204:212].rearrange("p (t g) -> p t g", t=TB), ST[:, 212:214]
                V(rk, B[7][:, 0:8].rearrange("p (t g) -> p t g", t=TB), hot, ALU.mult).then_inc(*vec.up())
                tot = ST[:, 216:220]
                eng.tensor_scalar(tot, B[7][:, 8:12], float(SLOTS), None, ALU.is_gt).then_inc(*vec.up())
                settle()
                eng.tensor_reduce(pos, rk, AX.X, ALU.add).then_inc(*vec.up())
                eng.tensor_reduce(ST[:, 222:223], tot, AX.X, ALU.add).then_inc(*vec.up())
                V(ST[:, 224:228], tot, iota4, ALU.mult).then_inc(*vec.up())
                settle()
                eng.tensor_reduce(ST[:, 223:224], ST[:, 224:228], AX.X, ALU.add).then_inc(*vec.up())
                late, gb = ST[:, 230:232], ST[:, 232:234]
                eng.tensor_scalar(late, pos, float(SLOTS), None, ALU.is_ge).then_inc(*vec.up())
                eng.tensor_scalar(gb, gid, 8.0, float(SLOTS), ALU.add, ALU.mult).then_inc(*vec.up())
                settle()
                V(pos, pos, gb, ALU.add).then_inc(*vec.up())
                eng.tensor_scalar(gb, gb, -1.0, float(SLOTS * (GROUPS - 1)), ALU.mult, ALU.add).then_inc(*vec.up())
                settle()
                V(gb, gb, late, ALU.mult).then_inc(*vec.up())
                settle()
                V(pos, pos, gb, ALU.add).then_inc(*vec.up())
                settle()
                eng.tensor_scalar(KEY[:, :], pos, float(SLOTS), None, ALU.add).then_inc(*vec.up())
                eng.tensor_copy(FLAG[:, :], ST[:, 222:224]).then_inc(plan_ready, 1)
                settle()

            STEPS = 10

            def experts_pass(m, P, used_at, l):
                steps = Count(m["steps"])

                def wait_steps():
                    eng.wait_ge(m["steps"], P * STEPS + steps.n)
                eng.tensor_scalar(KEY[:, :], KEY[:, :], -float(SLOTS), None, ALU.add).then_inc(*steps.up())
                wait_steps()
                eng.tensor_scalar(SEL[:, 0, :], iota, KEY[:, 0:1], None, ALU.is_equal).then_inc(*steps.up())
                eng.tensor_scalar(SEL[:, 1, :], iota, KEY[:, 1:2], None, ALU.is_equal).then_inc(m["slots_chosen"], 1)
                eng.wait_ge(m["gathered"], P * 2 + 2)
                for k in range(4, 8):
                    ins = eng.tensor_scalar(XG[:, k, :], B[1][:, (k - 4) * 128:(k - 3) * 128], SCL[:, 2 * l + 1, k:k + 1],
                                            MOD[:, l, 24 + k:25 + k], ALU.mult, ALU.add)
                    ins.then_inc(*(steps.up() if k < 7 else (m["feat_dve"], 1)))
                eng.wait_ge(m["slot_weights"], P + 1)
                eng.tensor_copy(WSL, B[2][:, 0:4]).then_inc(*steps.up())
                wait_steps()
                for e in range(4):
                    eng.wait_ge(m["silu"], P * 4 + (e + 1))
                    eng.wait_ge(m["used"], used_at("u", e))
                    if e >= 2:
                        eng.wait_ge(m["turned"], P * 4 + (e - 1))
                    eng.scalar_tensor_tensor(out=HE[e % 2], in0=SG[e % 2], scalar=WSL[:, e:e + 1],
                                             in1=B[5 + 2 * (e % 2)][:, :], op0=ALU.mult, op1=ALU.mult)\
                       .then_inc(m["hidden"], 1)
                eng.wait_ge(m["used"], used_at("d", 3))
                eng.tensor_copy(YE[:, 512:1024], B[1][:, :]).then_inc(m["y_dve"], 1)
                for c in range(4):
                    h, tb = c // 2, c % 2
                    eng.wait_ge(m["scattered"], P * 4 + (c + 1))
                    V(TMP[c % 2], B[4 + c][:, :], GB[:, 2 * l + 1, h * 512:(h + 1) * 512], ALU.mult).then_inc(*steps.up())
                    wait_steps()
                    xs = X[:, tb, h * 512:(h + 1) * 512]
                    V(xs, xs, TMP[c % 2], ALU.add).then_inc(m["added"], 1)
                assert steps.n == STEPS, steps.n

            def experts(l):
                route(l)
                first = tiles[st[f"moe{l}"]]["order"]
                with eng.Fori(0, PASSES) as p:
                    experts_pass(moe, p + PASSES * l, lambda kind, e: p * PASS_TILES + (first + PLACE[kind, e] + 1), l)
                eng.wait_ge(moe["added"], 16 * (l + 1) + 1)
                over = eng.value_load(FLAG[0:1, 0:1], min_val=0, max_val=1)
                with eng.If(over == 1):
                    eng.memset(FINI[:, :], 0.0).then_inc(ovf[l]["added"], 1)
                    experts_pass(ovf[l], 0, lambda kind, e: PLACE[kind, e] + 1, l)
                    eng.wait_ge(ovf[l]["added"], 5)
                finish_x()

            def feature(i):
                return HT[:, i, :]

            eng.memset(FINI[:, :], 0.0).then_inc(moe["added"], 1)
            normalise(lambda tb: PR[:, tb * D:(tb + 1) * D])
            eng.wait_ge(consts_loaded, CONSTS)
            V(bias, bias, bias, ALU.add).then_inc(*vec.up())
            settle()
            V(bias, bias, bias, ALU.add).then_inc(*vec.up())
            settle()
            eng.scalar_tensor_tensor(out=bias, in0=bias, scalar=2.0, in1=wide(chunk_mask.unsqueeze(1), 128, 8, 384),
                                     op0=ALU.mult, op1=ALU.add).then_inc(*vec.up())
            for l in range(2):
                take_turned(f"mem{l}", feature, lambda i, l=l: (GM[:, 10 + l, i:i + 1], None))
            eng.wait_ge(turned, turns["mem1"][0] + KD)
            eng.wait_ge(x_loaded, 16)
            norm_x()
            await_act()
            for j in range(12):
                ada_sum()
            ada_take(11)
            scales(0)
            eng.wait_ge(scales_ready, 2)
            take_turned("a0h1", feature, lambda i: (SCL[:, 0, i:i + 1], MOD[:, 0, i:i + 1]))
            for j in range(12):
                ada_sum()
            ada_take(23)
            scales(1)
            P0 = pview(EVEN_IN)
            eng.wait_ge(copied["act"], chunks[st["even_in"][-1][1][-1]]["done"])
            tmp = [NB[:, i // 2, (i % 2) * 512:(i % 2 + 1) * 512].rearrange("p (h n) -> p h n", h=8) for i in range(4)]
            for tb in range(TB):
                rotate(P0[:, tb, 0:1024].rearrange("p (h n) -> p h n", h=8), wide(cos_a[:, tb].unsqueeze(1), 128, 8, 64),
                       wide(sin_a[:, tb].unsqueeze(1), 128, 8, 64), 64, tmp)
            for tb in range(TB):
                q = P0[:, tb, 2048:3072]
                V(NB[:, tb, :], q, q, ALU.mult).then_inc(*vec.up())
            settle()
            for tb in range(TB):
                eng.tensor_reduce(VAR[:, 16 * tb:16 * tb + 16], NB[:, tb, :].rearrange("p (h n) -> p h n", h=16), AX.X,
                                  ALU.add).then_inc(*vec.up())
            settle()
            root(32, HD)
            for tb in range(TB):
                q = P0[:, tb, 2048:3072].rearrange("p (h n) -> p h n", h=16)
                ins = V(q, q, wide(RSD[:, 16 * tb:16 * tb + 16].unsqueeze(2), 128, 16, HD), ALU.mult)
            ins.then_inc(a0_rotated, 1)
            take_turned("a0ret", lambda i: QK[:, i, :])
            take_turned("a0att", lambda i: QK[:, 8 + i, :], lambda i: (AG[:, i // 4:i // 4 + 1], None))
            for h in range(RET_HEADS):
                eng.wait_ge(ret_scores, h + 1)
                V(SCR[:, h, :], B[h % 2][:, 0:384], decay[:, h, :], ALU.mult).then_inc(ret_decayed, 1)
            eng.wait_ge(ret_out, 4)
            sq = SCR[:, 4:8, :].rearrange("p a b -> p (a b)")[:, 0:1024]
            ret = NB[:, :, 0:512]
            V(sq.rearrange("p (t n) -> p t n", t=TB), ret, ret, ALU.mult).then_inc(*vec.up())
            settle()
            eng.tensor_reduce(VAR[:, 0:8], sq.rearrange("p (a n) -> p a n", n=128), AX.X, ALU.add).then_inc(*vec.up())
            settle()
            root(8, RET_DIM)
            for tb in range(TB):
                r = NB[:, tb, 0:512].rearrange("p (h n) -> p h n", h=4)
                V(r, r, wide(RSD[:, 4 * tb:4 * tb + 4].unsqueeze(2), 128, 4, 128), ALU.mult).then_inc(*vec.up())
            settle()
            await_act()
            V(ret, ret, P0[:, :, 1536:2048], ALU.mult).then_inc(*vec.up())
            settle()
            attention(units_of("a0", P0))
            eng.wait_ge(head_done, 16)
            eng.memset(FINI[:, :], 0.0).then_inc(a0_mixed, 1)
            take_turned("a0mix", feature)
            add_projected("even_out", 0, 1)
            norm_x()
            take_turned("a0h2", feature, lambda i: (SCL[:, 1, i:i + 1], MOD[:, 0, 24 + i:25 + i]))
            experts(0)

            norm_x()
            take_turned("a1h1", feature, lambda i: (SCL[:, 2, i:i + 1], MOD[:, 1, i:i + 1]))
            take_turned("a1qk", lambda i: QK[:, i, :])
            ZS = [AUX[:, 384 * i:384 * (i + 1)] for i in range(2)]
            LG = [AUX[:, 768 + 384 * i:1152 + 384 * i] for i in range(2)]
            WT = [AUX[:, 1536 + 384 * i:1920 + 384 * i] for i in range(2)]
            AE = [AUX[:, 2304 + 384 * i:2688 + 384 * i] for i in range(2)]
            for t in range(STICKS + 2):
                if t < STICKS:
                    eng.wait_ge(stick_log, t + 1)
                    if t >= 2:
                        eng.wait_ge(stick_exp, t - 1)
                        eng.wait_ge(stick_summed, t - 1)
                    z, g, w, L = ZS[t % 2], LG[t % 2], WT[t % 2], SCR[:, t % 2, :]
                    eng.scalar_tensor_tensor(out=w, in0=z, scalar=0.0, in1=g, op0=ALU.max, op1=ALU.add).then_inc(*vec.up())
                    settle()
                    V(L, w, strict, ALU.mult).then_inc(stick_logs, 1)
                    V(w, z, w, ALU.subtract).then_inc(*vec.up())
                if 1 <= t <= STICKS:
                    h = t - 1
                    eng.wait_ge(stick_summed, h + 1)
                    settle()
                    V(WT[h % 2], WT[h % 2], B[2 + h % 2][:, 0:384], ALU.subtract).then_inc(stick_arg, 1)
                if 1 <= t <= STICKS:
                    h = t - 1
                    eng.wait_ge(stick_exp, h + 1)
                    if h >= 2:
                        eng.wait_ge(stick_valued, h - 1)
                    V(SCR[:, 2 + h % 2, :], AE[h % 2], strict, ALU.mult).then_inc(stick_probs, 1)
            add_projected("odd_out", 2, 3)
            norm_x()
            take_turned("a1h2", feature, lambda i: (SCL[:, 3, i:i + 1], MOD[:, 1, 24 + i:25 + i]))
            experts(1)

            norm_x()
            take_turned("b0h0", feature, lambda i: (GM[:, 4, i:i + 1], None))
            P2 = pview(EV_IN)
            ANG, N_, CSB = SCR[:, 0, 0:32], SCR[:, 0, 32:64], SCR[:, 4, 0:32]
            a4 = ANG.rearrange("p (c t n) -> p c t n", c=2, t=TB)
            POSF = SCR[:, 0, 64:66]
            eng.tensor_copy(POSF, PI[:, :]).then_inc(*vec.up())
            settle()
            for c in range(2):
                V(a4[:, c], wide(POSF.unsqueeze(2), 128, TB, 8), wide(inv_freq.unsqueeze(1), 128, TB, 8), ALU.mult)\
                    .then_inc(*vec.up())
            settle()
            TWO_PI = 2.0 * np.pi
            MAGIC = 12582912.0
            c1 = 6.28125
            c2 = 0.0019350051879882812
            c3 = TWO_PI - c1 - c2
            for c in range(2):
                n_, x_ = N_.rearrange("p (c n) -> p c n", c=2)[:, c], ANG.rearrange("p (c n) -> p c n", c=2)[:, c]
                eng.tensor_scalar(n_, x_, 1.0 / TWO_PI, 0.25 * (1 - c), ALU.mult, ALU.add).then_inc(*vec.up())
            for op in (MAGIC, -MAGIC):
                settle()
                eng.tensor_scalar(N_, N_, op, None, ALU.add).then_inc(*vec.up())
            for c_ in (c1, c2, c3):
                settle()
                eng.scalar_tensor_tensor(out=ANG, in0=N_, scalar=-float(c_), in1=ANG, op0=ALU.mult, op1=ALU.add)\
                   .then_inc(*vec.up())
            settle()
            eng.tensor_scalar(ANG[:, 0:16], ANG[:, 0:16], float(np.pi / 2), None, ALU.add).then_inc(*vec.up())
            settle()
            eng.tensor_scalar(ANG, ANG, 3.1415925, -3.1415925, ALU.min, ALU.max).then_inc(ask_act, 1)
            await_act()
            await_act()
            cs = SCR[:, 0, 0:32].rearrange("p (c t n) -> p c t n", c=2, t=TB)
            eng.tensor_copy(ROPE[:, :, :, :], cs).then_inc(*vec.up())
            eng.wait_ge(copied["act"], chunks[st["ev_in"][-1][1][-1]]["done"])
            zf = SCR[:, 4, 0:16].rearrange("p (t n) -> p t n", t=TB)
            V(zf, P2[:, :, 1536:1544], wide(FB[:, :].unsqueeze(1), 128, TB, 8), ALU.add).then_inc(*vec.up())
            settle()
            az = SCR[:, 1, 0:16].rearrange("p (t n) -> p t n", t=TB)
            eng.scalar_tensor_tensor(out=az, in0=zf, scalar=-1.0, in1=zf, op0=ALU.mult, op1=ALU.max).then_inc(ask_act, 1)
            eng.memset(ST[:, 0:256], 0.0).then_inc(*vec.up())
            await_act()
            settle()
            LF = ST[:, 0:256].rearrange("p (t n) -> p t n", t=TB)
            for at in (0, 64):
                eng.scalar_tensor_tensor(out=LF[:, :, at:at + 8], in0=zf, scalar=0.0, in1=az, op0=ALU.min,
                                         op1=ALU.subtract).then_inc(*vec.up())
            T = [NB[:, i // 2, (i % 2) * 512:(i % 2 + 1) * 512] for i in range(4)]

            def rope_heads(P, at, count):
                for tb in range(TB):
                    v = P[:, tb, at:at + count * HD].rearrange("p (h n) -> p h n", h=count)
                    tmp = [x[:, 0:count * 8].rearrange("p (h n) -> p h n", h=count) for x in T]
                    rotate(v, wide(ROPE[:, 0, tb].unsqueeze(1), 128, count, 8),
                           wide(ROPE[:, 1, tb].unsqueeze(1), 128, count, 8), 8, tmp)
            rope_heads(P2, 1544, 10)
            rope_heads(P2, 2312, 2)
            rope_heads(P2, 2568, 2)
            KD4 = AUX[:, 4096:5120].rearrange("p (t x n) -> p t x n", t=TB, x=4)
            for tb in range(TB):
                for i in range(4):
                    at = (2312, 2568)[i // 2] + HD * (i % 2)
                    eng.tensor_copy(KD4[:, tb, i, :].rearrange("p (r n) -> p r n", r=2),
                                    wide(P2[:, tb, at:at + HD].unsqueeze(1), 128, 2, HD)).then_inc(*vec.up())
            settle()
            eng.memset(FINI[:, :], 0.0).then_inc(b0_roped, 1)
            take_turned("b0qk", lambda i: QK[:, i, :])
            XS = [AUX[:, 4096 + 496 * i:4592 + 496 * i].rearrange("p (k n) -> p k n", k=16) for i in range(2)]
            eng.wait_ge(cmp_pe, 1)
            for i in range(2):
                src = B[i][:, 0:256].rearrange("p (g c a) -> p a g c", g=2, a=8)
                for hi in range(2):
                    dst = XS[i][:, 8 * hi:8 * hi + 8, 0:30].rearrange("p a (g c) -> p a g c", g=2)
                    eng.tensor_copy(dst, src[:, :, :, hi:hi + CMP_N]).then_inc(*vec.up())
                eng.tensor_copy(XS[i][:, :, 30:31], POS[:, i, :].unsqueeze(2)).then_inc(*vec.up())
            settle()
            eng.memset(FINI[:, :], 0.0).then_inc(cmp_dve, 1)
            eng.wait_ge(weights_used, tiles[st["cmp"]]["order"] + 1)
            HCb, Hx = SCR[:, 0, 0:62], ST[:, 0:60]
            for i in range(2):
                eng.tensor_copy(HCb[:, 31 * i:31 * i + 31], B[2 + i][:, 0:31]).then_inc(*vec.up())
            settle()
            for i in range(2):
                eng.tensor_scalar(Hx[:, 30 * i:30 * i + 30], HCb[:, 31 * i:31 * i + 30], HCb[:, 31 * i + 30:31 * i + 31], None,
                                  ALU.add).then_inc(*vec.up())
            settle()
            u = ST[:, 60:120]
            V(u, Hx, Hx, ALU.mult).then_inc(*vec.up())
            settle()
            eng.tensor_scalar(u, u, 0.044715, 1.0, ALU.mult, ALU.add).then_inc(*vec.up())
            settle()
            V(u, u, Hx, ALU.mult).then_inc(cmp_dve, 1)
            eng.wait_ge(cmp_act, 1)
            eng.scalar_tensor_tensor(out=u, in0=u, scalar=1.0, in1=Hx, op0=ALU.add, op1=ALU.mult).then_inc(*vec.up())
            settle()
            eng.tensor_scalar(Hx, u, 0.5, None, ALU.mult).then_inc(cmp_dve, 1)
            eng.wait_ge(cmp_pe, 3)
            for g in range(2):
                V(VB[:, 256 * g:256 * (g + 1)].rearrange("p (n d) -> p n d", n=4),
                  wide(B[2][:, 64 * g:64 * (g + 1)].unsqueeze(1), 128, 4, HD),
                  wide(block_mask[:, 4 * g:4 * g + 4].unsqueeze(2), 128, 4, HD), ALU.mult).then_inc(*vec.up())
            CP4 = CP.rearrange("p t (h c) -> p t h c", c=16)
            eng.memset(CP, 0.0).then_inc(*vec.up())
            eng.wait_ge(cmp_pe, 4)
            settle()
            for par in range(2):
                for tb in range(TB):
                    eng.scalar_tensor_tensor(
                        out=CP4[:, tb, par::2, 0:CMP_N],
                        in0=B[4 + par][:, 64 * tb:64 * tb + 64].rearrange("p (h c) -> p h c", c=16)[:, :, 0:CMP_N],
                        scalar=HD ** -0.5, in1=wide(cmp_add[:, tb, 0:CMP_N].unsqueeze(1), 128, 4, CMP_N),
                        op0=ALU.mult, op1=ALU.add).then_inc(*vec.up())
            settle()
            mx, sm = SCR[:, 2, 0:16], SCR[:, 2, 16:32]
            CPh = CP.rearrange("p t (h c) -> p (t h) c", c=16)
            eng.tensor_reduce(mx, CPh[:, :, 0:CMP_N], AX.X, ALU.max).then_inc(*vec.up())
            settle()
            V(CPh, CPh, wide(mx.unsqueeze(2), 128, 16, 16), ALU.subtract).then_inc(*vec.up())
            settle()
            eng.memset(CPh[:, :, CMP_N:16], 0.0).then_inc(cmp_dve, 1)
            eng.wait_ge(cmp_act, 3)
            for tb in range(TB):
                V(CP4[:, tb], CP4[:, tb], wide(cmp_keep[:, tb].unsqueeze(1), 128, 8, 16), ALU.mult).then_inc(*vec.up())
            settle()
            eng.tensor_reduce(sm, CPh, AX.X, ALU.add).then_inc(*vec.up())
            settle()
            eng.tensor_scalar(sm, sm, 1e-30, None, ALU.max).then_inc(*vec.up())
            settle()
            eng.reciprocal(sm, sm).then_inc(*vec.up())
            settle()
            sm3 = sm.rearrange("p (t h) -> p t h", t=TB)
            V(sm3, sm3, GT.rearrange("p t (h b) -> p t h b", b=3)[:, :, :, 0], ALU.mult).then_inc(*vec.up())
            settle()
            V(CPh, CPh, wide(sm.unsqueeze(2), 128, 16, 16), ALU.mult).then_inc(cmp_dve, 1)
            eng.wait_ge(cmp_act, 5)
            attention(units_of("b0", P2))
            take_turned("b0mix", feature)

            def cross(l):
                norm_x()
                take_turned(f"b{l}h2", feature, lambda i: (GM[:, 5 + 3 * l, i:i + 1], None))
                attention(units_of(f"ca{l}", None))
                take_turned(f"b{l}ca", feature)
                add_normed_y(1)

            def feed_forward(l):
                norm_x()
                take_turned(f"b{l}h4", feature, lambda i: (GM[:, 6 + 3 * l, i:i + 1], None))
                n0 = 2 * FFN_STEPS * l
                order = tiles[st[f"ffn{l}"]]["order"]

                def hidden(s, par, up_used, free_at):
                    for f in range(2):
                        eng.wait_ge(ffn_silu, s * 2 + (n0 + f + 1))
                        if f == 0:
                            eng.wait_ge(ffn_up, s + (FFN_STEPS * l + 1))
                        else:
                            eng.wait_ge(weights_used, up_used)
                        if f == 0 and free_at is not None:
                            eng.wait_ge(weights_used, free_at)
                        V(FHE[2 * par + f], FSG[f], B[2 + f][:, 0:S], ALU.mult).then_inc(ffn_he, 1)
                hidden(0, 0, order + 1, None)
                with eng.Fori(0, (FFN_STEPS - 1) // 2) as i:
                    hidden(i * 2 + 1, 1, i * 4 + (order + 2), i * 4 + (order + 1))
                    hidden(i * 2 + 2, 0, i * 4 + (order + 4), i * 4 + (order + 3))
                add_normed_y(2)

            eng.wait_ge(gains_loaded, 16 * 3)
            add_normed_y(0)
            cross(0)
            feed_forward(0)

            norm_x()
            take_turned("b1h0", feature, lambda i: (GM[:, 7, i:i + 1], None))
            eng.wait_ge(gains_loaded, 16 * 7)
            lp = AUX[:, 3072:3328].rearrange("p (q n) -> p q n", q=4)
            for i in range(2):
                V(SCR[:, i, 0:HD], lp[:, 2 * i, :], lp[:, 2 * i + 1, :], ALU.mult).then_inc(*vec.up())
            settle()
            for i in range(2):
                eng.tensor_reduce(VAR[:, 30 + i:31 + i], SCR[:, i, 0:HD], AX.X, ALU.add)\
                   .then_inc(*((ask_act, 1) if i else vec.up()))
            await_act()
            V(LAM, VAR[:, 31:32], VAR[:, 30:31], ALU.subtract).then_inc(*vec.up())
            lam_init = 0.8 - 0.6 * float(np.exp(-0.3))
            settle()
            eng.tensor_scalar(LAM, LAM, -lam_init, None, ALU.add).then_inc(*vec.up())
            eng.tensor_scalar(AG[:, 2:3], AG[:, 2:3], 1.0 - lam_init, None, ALU.mult).then_inc(*vec.up())
            settle()
            P3 = pview(OD_IN)
            eng.wait_ge(copied["act"], chunks[st["od_in"][-1][1][-1]]["done"])
            rope_heads(P3, 0, 32)
            eng.memset(FINI[:, :], 0.0).then_inc(b1_roped, 1)
            take_turned("b1qk", lambda i: QK[:, i, :])
            attention(units_of("b1", P3))
            eng.wait_ge(head_done, UNITS["b1"][1])
            sq = PR[:, 0:2048]
            V(sq, NB[:, :, :].rearrange("p t n -> p (t n)"), NB[:, :, :].rearrange("p t n -> p (t n)"), ALU.mult)\
                .then_inc(*vec.up())
            settle()
            eng.tensor_reduce(VAR[:, 0:16], sq.rearrange("p (a n) -> p a n", n=128), AX.X, ALU.add).then_inc(*vec.up())
            settle()
            root(16, 128)
            nb = NB[:, :, :].rearrange("p t (h n) -> p (t h) n", n=128)
            V(nb, nb, wide(RSD[:, 0:16].unsqueeze(2), 128, 16, 128), ALU.mult).then_inc(b1_mixed, 1)
            take_turned("b1mix", feature, lambda i: (AG[:, 2:3], None))
            add_normed_y(0)
            cross(1)
            feed_forward(1)

        @block.gpsimd
        def _(eng):
            eng.wait_ge(x_ready, 3)
            for dst, src in ((possel[0:8], a["possel"]), (possel[64:72], a["possel"]),
                             (negsel[0:8], a["negsel"]), (negsel[64:72], a["negsel"])):
                eng.dma_start(dst, src).then_inc(aux_loaded, 16)
            for l in range(2):
                eng.wait_ge(x_ready, 4 + 3 * l)
                for i in range(3):
                    eng.dma_start(GB[:, i, :], a["sandwich_g_2"][l, 2 * i + 1, :].partition_broadcast(128))\
                       .then_inc(gains_loaded, 16)
                if l == 1:
                    eng.dma_start(AUX[:, 3072:3328],
                                  a["od_lambda_2"].rearrange("a q n -> (a q n)").partition_broadcast(128))\
                       .then_inc(gains_loaded, 16)


def consts_of_shapes():
    p = np.arange(128)
    f = np.float32
    lt = (p[:, None] < p[None, :]).astype(f)
    le = (p[:, None] <= p[None, :]).astype(f)
    one = np.ones((128, 128), f)
    causal = np.where(p[None, :] <= p[:, None], 0.0, NEG).astype(f)
    chunk0 = np.where(p[None, :] // CHUNK <= p[:, None] // CHUNK, 0.0, NEG).astype(f)
    inv = 10000.0 ** (-np.arange(0, RET_DIM, 2, dtype=f) / f(RET_DIM))
    ang = (np.arange(S, dtype=f)[:, None] * inv.astype(f)[None, :]).astype(f)
    fold = lambda t: t.reshape(TB, 128, -1).transpose(1, 0, 2).reshape(128, -1).astype(f)
    tok = np.arange(S)
    c = np.arange(16)
    keep = ((c[None, :] * 16 + 31 <= tok[:, None]) & (c[None, :] < CMP_N)).astype(f)
    invb = (500000.0 ** (-np.arange(0, 16, 2, dtype=f) / f(16))).astype(f)
    i4 = np.arange(4)
    low = np.broadcast_to((i4[None, :] < i4[:, None]).astype(f).reshape(1, 16), (128, 16))
    rep = np.zeros((128, 128), f)
    for h in range(8):
        for k in range(CMP_N):
            rep[k, h * 16 + k] = 1.0
    parts = [np.eye(128, dtype=f), lt, one, lt, le, (p[:, None] > p[None, :]).astype(f),
             np.broadcast_to(p.astype(f), (128, 128)), np.zeros((128, 256), f), causal,
             chunk0, np.zeros((128, 128), f), chunk0, fold(np.cos(ang)), fold(np.sin(ang)),
             (p[:, None] // 16 == np.arange(8)[None, :]).astype(f), fold(keep), fold((keep - 1.0) * f(-NEG)),
             np.broadcast_to(invb, (128, 8)), low, np.broadcast_to(i4.astype(f), (128, 4)), rep]
    consts = np.ascontiguousarray(np.concatenate(parts, axis=1), f)
    g = 1.0 - 2.0 ** (-5.0 - np.arange(RET_HEADS))
    i, j = np.arange(S)[None, :], np.arange(S)[:, None]
    d = np.where(i // CHUNK >= j // CHUNK, 1.0, 0.0) * g[:, None, None] ** np.abs(i - j) * RET_DIM ** -0.5
    decay = np.concatenate([d[:, 0:128, :], d[:, 128:256, 128:256]], axis=2).transpose(1, 0, 2)
    possel = np.zeros((8, 8, S), f)
    negsel = np.zeros((8, 8, 128), f)
    for h in range(8):
        possel[h, h] = HD ** 0.5
        negsel[h, h] = -HD ** 0.5
    return consts, np.ascontiguousarray(decay, f), possel, negsel


def features_first(v):
    v = np.asarray(v)
    return np.ascontiguousarray(v.reshape(v.shape[:-1] + (v.shape[-1] // 128, 128)).swapaxes(-1, -2))


BIG = ["x", "mem_2", "ada_w", "even_w_in", "even_w_out", "odd_w_in", "odd_w_out", "router_w", "router_b",
       "exp_w_gate", "exp_w_up", "exp_w_down", "sandwich_g_2", "ev_w_in_2", "ev_cmp_w1_k_2", "ev_cmp_w1_v_2",
       "ev_w_out_2", "od_w_in_2", "od_lambda_2", "od_w_out_2", "ca_wq_2", "ca_wk_2", "ca_wv_2", "ca_wo_2",
       "ffn_wg_2", "ffn_wu_2", "ffn_wd_2"]


def lay_out(inputs):
    z = {n: np.ascontiguousarray(inputs[n]) for n in BIG}
    g = lambda n: np.asarray(inputs[n])
    z["c_fm"] = features_first(g("c")[0])
    rows = [g("norm1_g")[0], g("norm2_g")[0], g("norm1_g")[1], g("norm2_g")[1]]
    rows += [g("sandwich_g_2")[l, i] for l in range(2) for i in (0, 2, 4)] + [g("mem_norm_g_2")[l] for l in range(2)]
    z["gains_fm"] = np.ascontiguousarray(features_first(np.stack(rows)).transpose(1, 0, 2))
    z["ada_b_fm"] = np.ascontiguousarray(features_first(g("ada_b")).transpose(1, 0, 2))
    z["gate_bias"] = np.ascontiguousarray(np.stack([g("ada_b")[l, 1024 * i:1024 * (i + 1)] for l in range(2) for i in (2, 5)]))
    twice = lambda v: np.concatenate([v, v])
    z["qk_gains"] = np.ascontiguousarray(np.stack([twice(g("att_q_norm_g")[0]), twice(g("att_k_norm_g")[0]),
                                                   g("od_subln_g_2")[0]], axis=1))
    z["cmp_pos"] = np.ascontiguousarray(np.stack([g(n)[0].reshape(16, 128).T for n in
                                                  ("ev_cmp_pos_k_2", "ev_cmp_pos_v_2")], axis=1))
    z["cmp_w2"] = np.ascontiguousarray(np.concatenate([g("ev_cmp_w2_k_2")[0], g("ev_cmp_w2_k_2")[0],
                                                       g("ev_cmp_w2_v_2")[0]], axis=1))
    at = np.clip(np.arange(S)[:, None] - np.arange(S)[None, :], -(CHUNK - 1), 128) + CHUNK - 1
    b = g("att_rel_bias")[0][:, at]
    z["rel_bias"] = np.ascontiguousarray(np.concatenate([b[:, 0:128, 0:128], b[:, 128:256, :]], axis=2).transpose(1, 0, 2))
    z["positions_fm"] = np.ascontiguousarray(g("positions_2")[0].reshape(TB, 128).T)
    z["fox_bias"] = np.ascontiguousarray(g("ev_fox_fbias_2")[0])
    z["consts"], z["decay"], z["possel"], z["negsel"] = consts_of_shapes()
    return z


def kernel(**inputs):
    import concourse.bacc as bacc
    from concourse.bass_utils import run_bass_kernel_spmd

    arrays = lay_out(inputs)
    nc = bacc.Bacc("TRN2", target_bir_lowering=False, num_devices=1)
    a = {n: nc.dram_tensor(f"in_{n}", v.shape, mybir.dt.from_np(v.dtype), kind="ExternalInput").ap()
         for n, v in arrays.items()}
    out = nc.dram_tensor("out_x", (1, S, D), F32, kind="ExternalOutput").ap()
    build(nc, a, out)
    r = run_bass_kernel_spmd(nc, [{f"in_{n}": v for n, v in arrays.items()}], core_ids=[0])
    return r.results[0]["out_x"]
```
